# Optimizing a Trainium2 kernel written in Bass

```python
import jax, jax.numpy as jnp
from jax import lax
import numpy as np

D_MODEL = 2048
BATCH = 1
SEQ = 512
DEPTH = 1

D_MIX = D_MODEL
N_MIXERS = 4
D_GROUP = D_MIX // N_MIXERS
HEAD_DIM = 128
N_HEADS = D_GROUP // HEAD_DIM
CHUNK = 128
CONV_WIDTH = 3
POOL_WINDOWS = (2, 4, 8, 16)
N_POOL = len(POOL_WINDOWS)
D_IN_PROJ = D_GROUP + 2 * D_GROUP + 3 * D_GROUP + D_GROUP
N_EXPERT_GROUPS = 4
EXPERTS_PER_GROUP = 8
N_EXPERTS = N_EXPERT_GROUPS * EXPERTS_PER_GROUP
TOP_K = 2
D_EXPERT = 768
MOE_BLOCK = 128
EPS = 1e-6

kernel_name = "hybrid_fourier_sgu_conv_pool_hmoe_encoder"

def rmsnorm(x, g):
    x32 = x.astype(jnp.float32)
    y = x32 * lax.rsqrt(jnp.mean(x32 * x32, axis=-1, keepdims=True) + EPS)
    return (y * g.astype(jnp.float32)).astype(x.dtype)

def fourier_mixer(z, w):
    b, s, _ = z.shape
    zh = z.astype(jnp.float32).reshape(b, s, N_HEADS, HEAD_DIM)
    f = jnp.fft.fft2(zh, axes=(1, 3), norm="ortho").real
    return f.reshape(b, s, D_GROUP).astype(z.dtype) @ w

def spatial_gating_mixer(z, w_s, b_s):
    b, s, _ = z.shape
    u, v = jnp.split(jax.nn.gelu(z, approximate=False), 2, axis=-1)
    v = v.reshape(b, s // CHUNK, CHUNK, N_HEADS, HEAD_DIM)
    mixed = jnp.einsum("hpq,bnqhc->bnphc", w_s, v) + b_s.T[None, None, :, :, None]
    return u * mixed.reshape(b, s, D_GROUP)

def short_conv_mixer(z, conv_w):
    gate_b, gate_c, val = jnp.split(z, 3, axis=-1)
    a = gate_c * val
    conv = lax.conv_general_dilated(
        a, conv_w[:, None, :], window_strides=(1,), padding=((1, 1),),
        dimension_numbers=("NWC", "WIO", "NWC"), feature_group_count=D_GROUP)
    return gate_b * conv

def multiscale_pool_mixer(z, w_pool, scale):
    b, s, _ = z.shape
    z32 = z.astype(jnp.float32)
    cs = jnp.concatenate([jnp.zeros((b, 1, D_GROUP), jnp.float32),
                          jnp.cumsum(z32, axis=1)], axis=1)
    t = jnp.arange(s)
    outs = []
    for g, w in enumerate(POOL_WINDOWS):
        lo = jnp.clip(t - w // 2, 0, s)
        hi = jnp.clip(t + w // 2, 0, s)
        sl = slice(g * HEAD_DIM, (g + 1) * HEAD_DIM)
        cg = cs[:, :, sl]
        count = (hi - lo).astype(jnp.float32)[None, :, None]
        mean = (jnp.take(cg, hi, axis=1) - jnp.take(cg, lo, axis=1)) / count
        outs.append(mean - z32[:, :, sl])
    p = jnp.stack(outs, axis=2).astype(z.dtype)
    y = jnp.einsum("bsgc,gcd->bsgd", p, w_pool).reshape(b, s, D_GROUP)
    return y * scale

def hierarchical_moe(h, w_group, b_group, w_router, b_router, w_gate, w_up, w_down):
    t, d = h.shape
    h32 = h.astype(jnp.float32)
    lg = h32 @ w_group.astype(jnp.float32) + b_group.astype(jnp.float32)
    pg = jax.nn.softmax(lg, axis=-1)
    grp = jnp.argmax(lg, axis=-1).astype(jnp.int32)
    p_grp = jnp.take_along_axis(pg, grp[:, None], axis=-1)
    le = (h32 @ w_router.astype(jnp.float32) + b_router.astype(jnp.float32))
    le = le.reshape(t, N_EXPERT_GROUPS, EXPERTS_PER_GROUP)
    le = jnp.take_along_axis(le, grp[:, None, None], axis=1)[:, 0]
    pe = jax.nn.softmax(le, axis=-1)
    top_p, top_i = lax.top_k(pe, TOP_K)
    gate = p_grp * top_p / jnp.sum(top_p, axis=-1, keepdims=True)
    expert = grp[:, None] * EXPERTS_PER_GROUP + top_i.astype(jnp.int32)

    n_assign = t * TOP_K
    flat_e = expert.reshape(-1)
    flat_tok = jnp.repeat(jnp.arange(t, dtype=jnp.int32), TOP_K)
    flat_gate = gate.reshape(-1)
    order = jnp.argsort(flat_e)
    sorted_e = flat_e[order]
    counts = jnp.bincount(flat_e, length=N_EXPERTS)
    padded = (counts + MOE_BLOCK - 1) // MOE_BLOCK * MOE_BLOCK
    pad_end = jnp.cumsum(padded)
    pad_start = pad_end - padded
    start = jnp.cumsum(counts) - counts
    dest = pad_start[sorted_e] + jnp.arange(n_assign) - start[sorted_e]
    n_rows = ((n_assign + MOE_BLOCK - 1) // MOE_BLOCK + N_EXPERTS) * MOE_BLOCK
    n_blocks = n_rows // MOE_BLOCK
    row_tok = jnp.full((n_rows,), t, jnp.int32).at[dest].set(flat_tok[order])
    row_gate = jnp.zeros((n_rows,), h.dtype).at[dest].set(flat_gate[order].astype(h.dtype))
    blk_exp = jnp.minimum(
        jnp.searchsorted(pad_end, jnp.arange(n_blocks) * MOE_BLOCK, side="right"),
        N_EXPERTS - 1)
    h_pad = jnp.concatenate([h, jnp.zeros((1, d), h.dtype)], axis=0)
    xb = h_pad[row_tok].reshape(n_blocks, MOE_BLOCK, d)

    def expert_block(args):
        xblk, e = args
        a = jax.nn.silu(xblk @ w_gate[e]) * (xblk @ w_up[e])
        return a @ w_down[e]

    yb = lax.map(expert_block, (xb, blk_exp)).reshape(n_rows, d)
    return jax.ops.segment_sum(yb * row_gate[:, None], row_tok, num_segments=t + 1)[:t]

def setup_inputs(seed: int = 0) -> dict:
    key = jax.random.key(seed)
    ks = jax.random.split(key, 20)
    f32 = jnp.float32
    L = DEPTH

    def nrm(k, shape, scale):
        return jax.random.normal(k, shape, f32) * scale

    return {
        "x": nrm(ks[0], (BATCH, SEQ, D_MODEL), 1.0),
        "mix_norm": 1.0 + nrm(ks[1], (L, D_MODEL), 0.02),
        "w_in": nrm(ks[2], (L, D_MODEL, D_IN_PROJ), D_MODEL ** -0.5),
        "w_fourier": nrm(ks[3], (L, D_GROUP, D_GROUP), D_GROUP ** -0.5),
        "w_spatial": nrm(ks[4], (L, N_HEADS, CHUNK, CHUNK), CHUNK ** -0.5),
        "b_spatial": 1.0 + nrm(ks[5], (L, N_HEADS, CHUNK), 0.1),
        "conv_w": nrm(ks[6], (L, CONV_WIDTH, D_GROUP), CONV_WIDTH ** -0.5),
        "w_pool": nrm(ks[7], (L, N_POOL, HEAD_DIM, HEAD_DIM), HEAD_DIM ** -0.5),
        "pool_scale": 1.0 + nrm(ks[8], (L, D_GROUP), 0.1),
        "out_norm": 1.0 + nrm(ks[9], (L, N_MIXERS, D_GROUP), 0.02),
        "w_out": nrm(ks[10], (L, D_MIX, D_MODEL), D_MIX ** -0.5),
        "ffn_norm": 1.0 + nrm(ks[11], (L, D_MODEL), 0.02),
        "w_group": nrm(ks[12], (L, D_MODEL, N_EXPERT_GROUPS), D_MODEL ** -0.5),
        "b_group": nrm(ks[13], (L, N_EXPERT_GROUPS), 0.01),
        "w_router": nrm(ks[14], (L, D_MODEL, N_EXPERTS), D_MODEL ** -0.5),
        "b_router": nrm(ks[15], (L, N_EXPERTS), 0.01),
        "w_gate": nrm(ks[16], (L, N_EXPERTS, D_MODEL, D_EXPERT), D_MODEL ** -0.5),
        "w_up": nrm(ks[17], (L, N_EXPERTS, D_MODEL, D_EXPERT), D_MODEL ** -0.5),
        "w_down": nrm(ks[18], (L, N_EXPERTS, D_EXPERT, D_MODEL), D_EXPERT ** -0.5),
        "final_norm": 1.0 + nrm(ks[19], (D_MODEL,), 0.02),
    }

def reference(x, mix_norm, w_in, w_fourier, w_spatial, b_spatial, conv_w, w_pool,
              pool_scale, out_norm, w_out, ffn_norm, w_group, b_group, w_router,
              b_router, w_gate, w_up, w_down, final_norm):
    b, s, d = x.shape
    for l in range(DEPTH):
        h = rmsnorm(x, mix_norm[l])
        z = h @ w_in[l]
        z_fourier = z[..., :D_GROUP]
        z_sgu = z[..., D_GROUP:3 * D_GROUP]
        z_conv = z[..., 3 * D_GROUP:6 * D_GROUP]
        z_pool = z[..., 6 * D_GROUP:]
        y = jnp.concatenate([
            fourier_mixer(z_fourier, w_fourier[l]),
            spatial_gating_mixer(z_sgu, w_spatial[l], b_spatial[l]),
            short_conv_mixer(z_conv, conv_w[l]),
            multiscale_pool_mixer(z_pool, w_pool[l], pool_scale[l]),
        ], axis=-1).reshape(b, s, N_MIXERS, D_GROUP)
        y = rmsnorm(y, out_norm[l]).reshape(b, s, D_MIX)
        x = x + y @ w_out[l]
        h = rmsnorm(x, ffn_norm[l]).reshape(b * s, d)
        x = x + hierarchical_moe(h, w_group[l], b_group[l], w_router[l], b_router[l],
                                 w_gate[l], w_up[l], w_down[l]).reshape(b, s, d)
    return rmsnorm(x, final_norm)


_drawn_inputs = setup_inputs


def setup_inputs(seed=0):
    import zlib

    import numpy as np

    out = dict(_drawn_inputs(seed))
    spreads = {}
    factors = {'ffn_norm': 2.684, 'b_group': 5.406, 'b_router': 6.74, 'final_norm': 2.912}
    for name, (base, spread) in spreads.items():
        noise = np.random.default_rng([zlib.crc32(name.encode()), seed]).standard_normal(out[name].shape)
        drawn = base * np.exp(spread * noise) if base else spread * noise
        out[name] = __import__('jax').numpy.asarray(drawn.astype(out[name].dtype))
    for name, factor in factors.items():
        out[name] = (out[name] * factor).astype(out[name].dtype)
    return out
```

```python
from contextlib import ExitStack

import concourse.bass as bass
import numpy as np
from concourse import mybir

F32 = mybir.dt.float32
I32 = mybir.dt.int32
U32 = mybir.dt.uint32
ALU = mybir.AluOpType
ACT = mybir.ActivationFunctionType
AX = mybir.AxisListType

P = 128
T = 512
D = 2048
DG = 512
HD = 128
NH = DG // HD
NT = T // P
KT = D // P
DIN = 7 * DG
NCH = DIN // DG
EPS = 1e-6
WINDOWS = (2, 4, 8, 16)
PAD = 8
POOLW = T + 2 * PAD

G = 4
EG = 8
E = G * EG
DE = 768
HF = DE // 2
FT = DE // P
SLOTS = 64
NSPLIT = T // SLOTS - 1
OVER = 2 * T // SLOTS
NA = 2 * NT
EMPTY = 4096.0
BIG = 1e30

QK = 4
NQ = KT // QK
GUS = 2 * NQ
DS = 3

C_MIX, C_OUT, C_SCALE, C_CONV, NCOL = 0, KT, 2 * KT, 2 * KT + NH, 2 * KT + NH + 3 * NH


def build(nc, x, mix_norm, w_in, w_fourier, w_spatial, b_spatial, conv_w, w_pool, pool_scale, out_norm,
          w_out, ffn_norm, w_group, b_group, w_router, b_router, w_gate, w_up, w_down, final_norm,
          dft_seq, dft_head, edge_scale, out):
    ctx = ExitStack()
    with ctx:
        def sem(name):
            return ctx.enter_context(nc.semaphore(name))

        KB = 256
        arena = ctx.enter_context(nc.sbuf_tensor("arena", [P, 53200], F32))
        ps = ctx.enter_context(nc.psum_tensor("banks", [P, 8, 512], F32))
        h2_dram = nc.dram_tensor("h2_rows", (T, D), F32).ap()
        moe_dram = nc.dram_tensor("moe_rows", (4 * T, D // 2), F32).ap()

        def at(off, *dims):
            n = int(np.prod(dims))
            v = arena[:, off:off + n]
            if len(dims) == 2:
                v = v.rearrange("p (a b) -> p a b", a=dims[0])
            if len(dims) == 3:
                v = v.rearrange("p (a b c) -> p a b c", a=dims[0], b=dims[1])
            if len(dims) == 4:
                v = v.rearrange("p (a b c d) -> p a b c d", a=dims[0], b=dims[1], c=dims[2])
            return v

        X, H, W0, W1, Z, DFT, CD, SM = (k * KB for k in (0, 32, 64, 96, 128, 184, 200, 201))

        x_sb = at(X, NT, D)
        hT = at(H, KT, T)
        yT = at(H, KT, T)
        wbuf = [at(W0, KT, DG), at(W1, KT, DG)]
        zT = at(Z, NCH * NH, T)
        rows = at(Z + 27 * T, P)
        junk = at(Z, D)
        dft = at(DFT, 2, NT, T)
        dfth = at(CD, 2 * HD)
        wf = at(X, NH, DG)
        ab = at(X + 8 * KB, NT, NH, 2 * HD)
        vq = at(X + 24 * KB, NH, NT, HD)
        fT = at(Z, NH, T)
        rstd = at(Z + 16 * T, NH, T)
        o = W1
        ws_raw = at(o, NH, P)
        wsT = at(o + 512, NH, P)
        wp = at(o + 1024, NH, HD)
        bsp = at(o + 1536, NH, P)
        pool_in = at(o + 2048, POOLW)
        pool_a = at(o + 2048 + POOLW, POOLW)
        pool_b = at(o + 2048 + 2 * POOLW, POOLW)
        o2 = o + 2048 + 3 * POOLW
        conv_a = at(o2, T + 2)
        conv_t = at(o2 + 514, T)
        edges = at(o2 + 514 + T, NH, 2, PAD)
        sq = at(o2 + 514 + T + 64, NH, T)
        assert o2 + 514 + T + 64 + NH * T <= Z

        o = SM
        ident = at(o, P); o += P
        mean_w = at(o, P); o += P
        ones = at(o, P); o += P
        before = at(o, P); o += P
        wr = at(o, KT, G + E); o += KT * (G + E)
        cols = at(o, NCOL); o += NCOL
        bias36 = at(o, G + E); o += G + E
        iota64 = at(o, P); o += P
        stat = at(o, 24); o += 24
        eps = at(o, 1); o += 1
        pri4 = at(o, G); o += G
        pri8 = at(o, EG); o += EG
        e64 = at(o, E); o += E
        thr = at(o, NSPLIT); o += NSPLIT
        nums = at(o, OVER); o += OVER
        asg = at(o, NT, 2, 4); o += NA * 4
        slot = at(o, NT, 2); o += NA
        half = at(o, 1); o += 1
        gidx = [at(o + k, 1).bitcast(U32) for k in (0, 1)]; o += 2
        sidx = [at(o + k, 1).bitcast(U32) for k in (0, 1)]; o += 2
        gate = [at(o + k, 1) for k in (0, 1)]; o += 2
        over_f = at(o, OVER + 1); o += OVER + 1
        over_i = at(o, OVER + 1).bitcast(I32); o += OVER + 1
        assert o <= 53200, o

        ffn_row = at(188 * KB, D)
        h2 = [at(W0, D), at(W0 + 8 * KB, D)]
        h2T = at(W0 + 16 * KB, KT, P)
        junk2 = at(W0 + 24 * KB, D)
        gu = [at(Z + s * 12 * KB, QK, DE) for s in range(5)] + [at(H, QK, DE), at(H + 12 * KB, QK, DE),
                                                               at(W0, QK, DE)]
        hg = at(H + 24 * KB, D)
        yg = [at(W0 + 12 * KB, D // 2), at(W0 + 16 * KB, D // 2)]
        pick = at(W0 + 20 * KB, NA, P)
        aT = at(W0 + 24 * KB, HF // P, P)
        sg = at(W0 + 24 * KB + HF, HF)
        act = at(W0 + 24 * KB + 2 * HF, HF)
        wd = [at(W1 + s * 8 * KB, D) for s in range(DS)]
        hTe = at(W1 + 24 * KB, KT, SLOTS)
        y_rows = [[at(Z + (2 * t + k) * 8 * KB, D) for k in (0, 1)] for t in range(NT)]
        final_row = at(H, D)
        o = W1 + 24 * KB
        lg = at(o, NT, G + E); o += NT * (G + E)
        prod = at(o, NT, G, EG); o += NT * E
        both = at(o, NT, 2, E); o += NT * 2 * E
        full = at(o, 2, NT, E); o += 2 * NT * E
        A = at(o, NT, E); o += NT * E
        tot = at(o, NT, E); o += NT * E
        Q = at(o, NT, E); o += NT * E
        t1 = at(o, NT, E); o += NT * E
        les = at(o, NT, EG); o += NT * EG
        les2 = at(o, NT, EG); o += NT * EG
        r8 = at(o, NT, EG); o += NT * EG
        oh = at(o, 2, NT, EG); o += 2 * NT * EG
        ohg = at(o, NT, G); o += NT * G
        lgm = at(o, NT, G); o += NT * G
        r4 = at(o, NT, G); o += NT * G
        v4 = at(o, 12, NT); o += 12 * NT
        extra = at(o, E); o += E
        over_end = at(o, E); o += E
        over_v = at(o, E); o += E
        assert o <= Z, (o, Z)
        split_cmp = at(W0 + 12 * KB, E, NSPLIT)
        id_cmp = at(W0 + 13 * KB, OVER, E)
        zero32 = at(W0 + 15 * KB, E)

        win_v = w_in[0].rearrange("(k p) n -> p k n", p=P)
        wout_v = w_out[0].rearrange("(k p) n -> p k n", p=P)
        wg_v = w_gate[0].rearrange("e (p k) n -> e p k n", k=KT)
        wu_v = w_up[0].rearrange("e (p k) n -> e p k n", k=KT)
        wdn_v = w_down[0].rearrange("e (k p) n -> e p k n", p=P)
        x_v = x[0].rearrange("(t p) n -> p t n", p=P)
        out_v = out[0].rearrange("(t p) n -> p t n", p=P)
        moe_v = moe_dram.rearrange("(k t p c) n -> k t p (c n)", k=2, t=NT, p=P, c=2)

        x_landed = [sem(f"x_landed{t}") for t in range(NT)]
        rows_landed = sem("rows_landed")
        dft_landed = sem("dft_landed")
        router_landed = sem("router_landed")
        mixw_landed = sem("mixw_landed")
        w_landed = [sem("w_landed0"), sem("w_landed1")]
        x_back = sem("x_back")
        ffn_landed = sem("ffn_landed")
        final_landed = sem("final_landed")
        gu_landed = [sem(f"gu_landed{s}") for s in range(GUS)]
        wd_landed = [sem(f"wd_landed{s}") for s in range(DS)]
        consts = sem("consts")
        cols_ps, cols_ready = sem("cols_ps"), sem("cols_ready")
        x_sq, x_rms, x_rinv, xn_ready = sem("x_sq"), sem("x_rms"), sem("x_rinv"), sem("xn_ready")
        ht_ps, ht_stored = sem("ht_ps"), sem("ht_stored")
        z_ps, z_stored = sem("z_ps"), sem("z_stored")
        v_gelu, u_gelu = sem("v_gelu"), sem("u_gelu")
        ab_ps, ab_stored = sem("ab_ps"), sem("ab_stored")
        vq_ps, vq_stored = sem("vq_ps"), sem("vq_stored")
        ws_ps, ws_stored = sem("ws_ps"), sem("ws_stored")
        ft_ps, ft_stored = sem("ft_ps"), sem("ft_stored")
        mix_ps, mix_stored = sem("mix_ps"), sem("mix_stored")
        pooled, pool_ps, pool_stored = sem("pooled"), sem("pool_ps"), sem("pool_stored")
        conv_stored = sem("conv_stored")
        yf_ps, yf_stored = sem("yf_ps"), sem("yf_stored")
        sq_ready, ms_ps, rms_ready, y_normed = sem("sq_ready"), sem("ms_ps"), sem("rms_ready"), sem("y_normed")
        xo_ps, x2_stored = sem("xo_ps"), sem("x2_stored")
        x2_sq, x2_rms, x2_rinv, h2_ready = sem("x2_sq"), sem("x2_rms"), sem("x2_rinv"), sem("h2_ready")
        h2_saved = [sem("h2_saved0"), sem("h2_saved1")]
        h2t_ps, h2t_act, h2t_dve = sem("h2t_ps"), sem("h2t_act"), sem("h2t_dve")
        logits_ps = sem("logits_ps")
        exp_in, exp_out, routed, counted = sem("exp_in"), sem("exp_out"), sem("routed"), sem("counted")
        pick_ready, plan_ps, plan_read, idx_ready = sem("pick_ready"), sem("plan_ps"), sem("plan_read"), sem("idx_ready")
        slots_shifted = sem("slots_shifted")
        rows_gathered = sem("rows_gathered")
        hte_ps, hte_ready = sem("hte_ps"), sem("hte_ready")
        gu_used = [sem(f"gu_used{s}") for s in range(GUS)]
        silu_ready, act_ready = sem("silu_ready"), sem("act_ready")
        at_ps, at_ready = sem("at_ps"), sem("at_ready")
        wd_used = [sem(f"wd_used{s}") for s in range(DS)]
        yg_ready = sem("yg_ready")
        yg_sent = [sem("yg_sent0"), sem("yg_sent1")]
        y_landed = [sem(f"y_landed{t}") for t in range(NT)]
        summed, f_rms, f_rinv, out_ready = sem("summed"), sem("f_rms"), sem("f_rinv"), sem("out_ready")
        out_saved = sem("out_saved")
        dve_done, act_done = sem("dve_done"), sem("act_done")
        turns = sem("turns")

        Z_FREE = 8
        OUT_TILES = NT * 4
        MIX_TILES = KT

        block = ctx.enter_context(nc.Block())

        @block.sync
        def _(sp):
            for t in range(NT):
                sp.dma_start(x_sb[:, t, :], x_v[:, t, :]).then_inc(x_landed[t], 16)
            for b in (0, 1):
                sp.dma_start(wbuf[b], win_v[:, :, b * DG:(b + 1) * DG]).then_inc(w_landed[b], 16)
            with sp.Fori(1, 3) as i:
                for b in (0, 1):
                    sp.wait_ge(z_ps, i * 8 + (4 * b - 4))
                    sp.dma_start(wbuf[b], win_v[:, :, bass.ds(i * (2 * DG) + b * DG, DG)]).then_inc(w_landed[b], 16)
            sp.wait_ge(z_ps, 20)
            sp.dma_start(wbuf[0], win_v[:, :, 6 * DG:]).then_inc(w_landed[0], 16)
            sp.wait_ge(ht_ps, 16)
            sp.dma_start(wf, w_fourier[0].rearrange("(k p) n -> p k n", p=P)).then_inc(mixw_landed, 16)
            sp.wait_ge(z_ps, 24)
            sp.dma_start(ws_raw, w_spatial[0].rearrange("h p q -> p h q")).then_inc(mixw_landed, 16)
            sp.dma_start(wp, w_pool[0].rearrange("g c d -> c g d")).then_inc(mixw_landed, 16)
            sp.dma_start(bsp[0:1], b_spatial).then_inc(mixw_landed, 16)
            sp.dma_start(edges.rearrange("p a b c -> p (a b c)"), edge_scale).then_inc(mixw_landed, 16)
            sp.wait_ge(z_ps, 28)
            sp.dma_start(wbuf[0], wout_v[:, :, 0:DG]).then_inc(w_landed[0], 16)
            sp.wait_ge(y_normed, MIX_TILES)
            sp.dma_start(x_sb, x_v).then_inc(x_back, 16)
            sp.dma_start(wbuf[1], wout_v[:, :, DG:2 * DG]).then_inc(w_landed[1], 16)
            sp.dma_start(ffn_row, ffn_norm.to_broadcast([P, D])).then_inc(ffn_landed, 16)

            def gate_up(e, s):
                src = (wg_v, wu_v)[s % 2]
                q = s // 2
                sp.dma_start(gu[s], src[e, :, q * QK:(q + 1) * QK, :]).then_inc(gu_landed[s], 16)

            def down(e, k):
                sp.dma_start(wd[k % DS], wdn_v[e, :, k, :]).then_inc(wd_landed[k % DS], 16)

            for s in range(4):
                gate_up(0, s)
            sp.wait_ge(xo_ps, 4)
            sp.dma_start(wbuf[0], wout_v[:, :, 2 * DG:3 * DG]).then_inc(w_landed[0], 16)
            gate_up(0, 4)
            sp.wait_ge(xo_ps, 8)
            sp.dma_start(wbuf[1], wout_v[:, :, 3 * DG:4 * DG]).then_inc(w_landed[1], 16)
            sp.wait_ge(xo_ps, OUT_TILES)
            gate_up(0, 5)
            gate_up(0, 6)
            for k in range(DS):
                down(0, k)
            sp.wait_ge(h2t_ps, 16)
            for b in (0, 1):
                sp.wait_ge(h2_saved[b], 32)
            gate_up(0, 7)
            for k in range(DS, FT):
                sp.wait_ge(wd_used[k % DS], 1)
                down(0, k)

            def weights(e, expert):
                for s in range(GUS):
                    sp.wait_ge(gu_used[s], e)
                    gate_up(expert, s)
                for k in range(FT):
                    sp.wait_ge(wd_used[k % DS], e * 2 + k // DS)
                    down(expert, k)

            with sp.Fori(1, E) as e:
                weights(e, e)
            sp.wait_ge(counted, 1)
            n_over = sp.value_load(over_i[0:1, OVER:OVER + 1], min_val=0, max_val=OVER)
            with sp.If(n_over > 0):
                with sp.Fori(0, OVER) as j:
                    expert = sp.value_load(over_i[0:1, bass.ds(j, 1)], min_val=0, max_val=E - 1)
                    weights(j + E, expert)
                for b in (0, 1):
                    sp.wait_ge(yg_sent[b], 16 * (E + OVER) // 2)
            for b in (0, 1):
                sp.wait_ge(yg_sent[b], 16 * E // 2)
            sp.dma_start(final_row, final_norm.rearrange("(a n) -> a n", a=1).to_broadcast([P, D])).then_inc(final_landed, 16)
            for t in range(NT):
                for k in (0, 1):
                    sp.dma_start(y_rows[t][k], moe_v[k, t]).then_inc(y_landed[t], 16)
            for t in range(NT):
                sp.wait_ge(out_ready, t + 1)
                sp.dma_start(out_v[:, t, :], x_sb[:, t, :]).then_inc(out_saved, 16)
            sp.wait_ge(out_saved, 16 * NT)

        @block.gpsimd
        def _(pool):
            n = 0

            def made(ins):
                nonlocal n
                n += 1
                ins.then_inc(consts, 1)
                pool.wait_ge(consts, n)

            g = nc.gpsimd
            made(g.memset(ident, 0.0))
            made(g.affine_select(out=ident, in_=ident, compare_op=ALU.not_equal, fill=1.0, base=0,
                                 pattern=[[-1, P]], channel_multiplier=1))
            made(g.memset(mean_w, 1.0 / DG))
            made(g.memset(eps, EPS))
            made(g.memset(ones, 1.0))
            made(g.affine_select(out=before, in_=ones, compare_op=ALU.is_gt, fill=0.0, base=0,
                                 pattern=[[1, P]], channel_multiplier=-1))
            made(g.iota(iota64.rearrange("p (a b) -> p a b", a=2), [[0, 2], [1, SLOTS]], 0, 0,
                        allow_small_or_imprecise_dtypes=True))
            made(g.iota(pri4, [[-1, G]], G, 0, allow_small_or_imprecise_dtypes=True))
            made(g.iota(pri8, [[-1, EG]], EG, 0, allow_small_or_imprecise_dtypes=True))
            made(g.iota(e64, [[SLOTS, E]], 0, 0, allow_small_or_imprecise_dtypes=True))
            made(g.iota(thr, [[SLOTS, NSPLIT]], SLOTS, 0, allow_small_or_imprecise_dtypes=True))
            made(g.iota(nums, [[1, OVER]], 0, 0, allow_small_or_imprecise_dtypes=True))
            made(g.iota(asg[:, :, :, 0], [[P, NT], [0, 2]], 0, 1, allow_small_or_imprecise_dtypes=True))
            made(g.iota(asg[:, :, :, 2], [[2 * P, NT], [2 * T, 2]], -int(EMPTY), 2, allow_small_or_imprecise_dtypes=True))
            made(g.memset(half, EMPTY))
            made(g.memset(half[P // 2:P], EMPTY + 1))

            def gather(e, b, first=False):
                pool.wait_ge(idx_ready, e + 1)
                if not first:
                    pool.wait_ge(hte_ps, e)
                pool.sem_inc(turns, 1)
                g.indirect_dma_start(out=hg[0:SLOTS], out_offset=None, in_=h2_dram,
                                     in_offset=bass.IndirectOffsetOnAxis(ap=gidx[b][0:SLOTS], axis=0))\
                    .then_inc(rows_gathered, 16)

            def scatter(e, b):
                pool.wait_ge(yg_ready, e + 1)
                pool.sem_inc(turns, 1)
                g.indirect_dma_start(out=moe_dram, out_offset=bass.IndirectOffsetOnAxis(ap=sidx[b], axis=0),
                                     in_=yg[b], in_offset=None, bounds_check=4 * T - 1, oob_is_err=False)\
                    .then_inc(yg_sent[b], 16)

            for b in (0, 1):
                pool.wait_ge(h2_saved[b], 32)
            gather(0, 0, first=True)

            def blocks(i):
                for b in (0, 1):
                    gather(i * 2 + (b + 1), 1 - b)
                    scatter(i * 2 + b, b)

            with pool.Fori(0, E // 2) as i:
                blocks(i)
            n_over = pool.value_load(over_i[0:1, OVER:OVER + 1], min_val=0, max_val=OVER)
            with pool.If(n_over > 0):
                with pool.Fori(E // 2, (E + OVER) // 2) as i:
                    blocks(i)
                pool.wait_ge(rows_gathered, 16 * (E + OVER + 1))
            pool.wait_ge(rows_gathered, 16 * (E + 1))

        @block.scalar
        def _(ae):
            a = nc.scalar
            ae.dma_start(rows[0:KT], mix_norm[0].rearrange("(r c) -> r c", c=P)).then_inc(rows_landed, 16)
            ae.dma_start(rows[C_OUT:C_OUT + KT], out_norm[0].rearrange("m (r c) -> (m r) c", c=P)).then_inc(rows_landed, 16)
            ae.dma_start(rows[C_SCALE:C_SCALE + NH], pool_scale[0].rearrange("(r c) -> r c", c=P)).then_inc(rows_landed, 16)
            ae.dma_start(rows[C_CONV:NCOL], conv_w[0].rearrange("w (r c) -> (w r) c", c=P)).then_inc(rows_landed, 16)
            ae.dma_start(dft, dft_seq.rearrange("c (t p) n -> p c t n", p=P)).then_inc(dft_landed, 16)
            ae.dma_start(dfth, dft_head).then_inc(dft_landed, 16)
            ae.dma_start(wr[:, :, 0:G], w_group[0].rearrange("(p k) n -> p k n", k=KT)).then_inc(router_landed, 16)
            ae.dma_start(wr[:, :, G:], w_router[0].rearrange("(p k) n -> p k n", k=KT)).then_inc(router_landed, 16)
            ae.dma_start(bias36[:, 0:G], b_group.to_broadcast([P, G])).then_inc(router_landed, 16)
            ae.dma_start(bias36[:, G:], b_router.to_broadcast([P, E])).then_inc(router_landed, 16)

            ae.wait_ge(consts, 4)
            for t in range(NT):
                ae.wait_ge(x_landed[t], 16)
                if t:
                    ae.wait_ge(x_sq, t)
                a.activation(junk, x_sb[:, t, :], ACT.Square, accum_out=stat[:, t:t + 1]).then_inc(x_sq, 1)
                ae.wait_ge(x_sq, t + 1)
                a.activation(stat[:, NT + t:NT + t + 1], stat[:, t:t + 1], ACT.Sqrt, bias=eps, scale=1.0 / D)\
                    .then_inc(x_rms, 1)

            ae.sem_inc(z_stored, Z_FREE)

            def store_z(nth, dst, bank):
                ae.wait_ge(z_ps, nth)
                a.activation(dst, ps[:, bank, :], ACT.Copy).then_inc(z_stored, 1)

            with ae.Fori(0, 3) as i:
                for j in range(8):
                    store_z(i * 8 + (j + 1), zT[:, bass.ds(i * 8 + j, 1), :].rearrange("p a b -> p (a b)"), j)
            for j in range(4):
                store_z(25 + j, zT[:, 24 + j, :], j)

            ae.wait_ge(z_stored, Z_FREE + 28)
            for h in range(NH):
                a.activation(zT[:, 8 + h, :], zT[:, 8 + h, :], ACT.Gelu).then_inc(v_gelu, 1)
            for h in range(NH):
                a.activation(zT[:, 4 + h, :], zT[:, 4 + h, :], ACT.Gelu).then_inc(u_gelu, 1)
            for h in range(NH):
                ae.wait_ge(vq_ps, h + 1)
                a.activation(vq[:, h].rearrange("p n c -> p (n c)"), ps[:, 4 + h, :], ACT.Copy).then_inc(vq_stored, 1)
            for h in range(NH):
                ae.wait_ge(ft_ps, h + 1)
                a.activation(fT[:, h, :], ps[:, (h + 1) % 4, :], ACT.Copy).then_inc(ft_stored, 1)

            def squares(group, done, count):
                ae.wait_ge(done, count)
                if group_order.index(group):
                    ae.wait_ge(ms_ps, group_order.index(group))
                for m in range(NH):
                    a.activation(sq[:, m, :], yT[:, group * NH + m, :], ACT.Square).then_inc(sq_ready, 1)

            group_order = [2, 3, 1, 0]
            squares(2, conv_stored, 4)
            for g in range(NH):
                ae.wait_ge(pool_ps, g + 1)
                a.activation(yT[:, 12 + g, :], ps[:, g, :], ACT.Copy, scale=cols[:, C_SCALE + g:C_SCALE + g + 1])\
                    .then_inc(pool_stored, 1)
            squares(3, pool_stored, 4)
            for m in (0, 1):
                ae.wait_ge(yf_ps, m + 1)
                a.activation(yT[:, m, :], ps[:, m, :], ACT.Copy).then_inc(yf_stored, 1)
            squares(1, mix_stored, 4)
            for m in (2, 3):
                ae.wait_ge(yf_ps, m + 1)
                a.activation(yT[:, m, :], ps[:, m, :], ACT.Copy).then_inc(yf_stored, 1)
            squares(0, yf_stored, 4)
            for n_, group in enumerate(group_order):
                ae.wait_ge(ms_ps, n_ + 1)
                a.activation(rstd[:, n_, :], ps[:, 4 + n_, :], ACT.Sqrt, bias=eps).then_inc(rms_ready, 1)

            for t in range(NT):
                ae.wait_ge(x2_stored, Z_FREE + 12 + t + 1)
                if t:
                    ae.wait_ge(x2_sq, t)
                else:
                    ae.wait_ge(xo_ps, 12)
                a.activation(junk2, x_sb[:, t, :], ACT.Square, accum_out=stat[:, 12 + t:13 + t]).then_inc(x2_sq, 1)
                ae.wait_ge(x2_sq, t + 1)
                a.activation(stat[:, 16 + t:17 + t], stat[:, 12 + t:13 + t], ACT.Sqrt, bias=eps, scale=1.0 / D)\
                    .then_inc(x2_rms, 1)
                ae.wait_ge(h2_ready, t + 1)
                ae.dma_start(h2_dram[t * P:(t + 1) * P, :], h2[t % 2]).then_inc(h2_saved[t % 2], 16)
                for q in (0, 1):
                    ae.wait_ge(h2t_ps, 4 * t + q + 1)
                    if t:
                        ae.wait_ge(logits_ps, t)
                    a.activation(h2T[:, 4 * q:4 * q + 4, :].rearrange("p a b -> p (a b)"), ps[:, q, :], ACT.Copy)\
                        .then_inc(h2t_act, 1)
            ae.wait_ge(exp_in, 1)
            a.activation(lgm, lgm, ACT.Exp).then_inc(exp_out, 1)
            ae.wait_ge(exp_in, 2)
            a.activation(v4[:, 5, :], v4[:, 5, :], ACT.Exp).then_inc(exp_out, 1)

            def store_rows_T(e):
                ae.wait_ge(hte_ps, e + 1)
                a.activation(hTe.rearrange("p (a b) c -> p a (b c)", a=2), ps[:, 2:4, :], ACT.Copy).then_inc(hte_ready, 1)

            def blocks(i, first=False):
                for b in (0, 1):
                    e = i * 2 + b
                    ae.wait_ge(gu_used[GUS - 2], e + 1)
                    a.activation(sg, ps[:, 0, 0:HF], ACT.Silu).then_inc(silu_ready, 1)
                    store_rows_T(e + 1)
                    ae.wait_ge(wd_used[DS - 1], e * 2 + 2)
                    if not first:
                        ae.wait_ge(yg_sent[b], i * 16)
                    a.activation(yg[b].rearrange("p (a c) -> p a c", a=2), ps[:, 5:7, :], ACT.Copy,
                                 scale=gate[b]).then_inc(yg_ready, 1)

            store_rows_T(0)
            blocks(0, first=True)
            with ae.Fori(1, E // 2) as i:
                blocks(i)
            ae.wait_ge(counted, 1)
            n_over = ae.value_load(over_i[0:1, OVER:OVER + 1], min_val=0, max_val=OVER)
            with ae.If(n_over > 0):
                with ae.Fori(E // 2, (E + OVER) // 2) as i:
                    blocks(i)
                ae.wait_ge(yg_ready, E + OVER)
            ae.wait_ge(yg_ready, E)

            for t in range(NT):
                ae.wait_ge(summed, 2 * t + 2)
                a.activation(y_rows[t][0], x_sb[:, t, :], ACT.Square, accum_out=stat[:, t:t + 1]).then_inc(act_done, 1)
                ae.wait_ge(act_done, t + 1)
                a.activation(stat[:, NT + t:NT + t + 1], stat[:, t:t + 1], ACT.Sqrt, bias=eps, scale=1.0 / D)\
                    .then_inc(f_rms, 1)

        @block.tensor
        def _(pe):
            t_ = nc.tensor
            pe.wait_ge(consts, 2)
            pe.wait_ge(rows_landed, 64)
            t_.transpose(ps[:, 7, 0:NCOL], rows[0:NCOL], ident[0:NCOL, 0:NCOL]).then_inc(cols_ps, 1)

            for t in range(NT):
                pe.wait_ge(xn_ready, t + 1)
                for q in range(4):
                    if t >= 2:
                        pe.wait_ge(ht_stored, (t - 2) * 4 + q + 1)
                    elif t == 1 and q == 3:
                        pe.wait_ge(cols_ready, 1)
                    for k in range(4):
                        c = (4 * q + k) * P
                        mm = t_.transpose(ps[:, (4 * t + q) % 8, k * P:(k + 1) * P], x_sb[:, t, c:c + P], ident)
                    mm.then_inc(ht_ps, 1)

            pe.wait_ge(consts, 16)
            pe.wait_ge(ht_stored, 4 * NT)

            def project(w, b, nth):
                pe.wait_ge(w_landed[b], w)
                for m in range(4):
                    pe.wait_ge(z_stored, nth + m)
                    for k in range(KT):
                        mm = t_.matmul(ps[:, 4 * b + m, :], wbuf[b][:, k, m * P:(m + 1) * P], hT[:, k, :],
                                       start=(k == 0), stop=(k == KT - 1))
                    mm.then_inc(z_ps, 1)

            with pe.Fori(0, 3) as i:
                for b in (0, 1):
                    project(i * 16 + 16, b, i * 8 + (4 * b + 1))
            project(64, 0, 25)

            pe.wait_ge(dft_landed, 32)
            for s in range(NT):
                if s < 2:
                    pe.wait_ge(z_stored, Z_FREE + 24)
                else:
                    pe.wait_ge(ab_stored, s - 1)
                for h in range(NH):
                    c = (h % 2) * 2 * HD
                    mm = t_.matmul(ps[:, 4 + 2 * (s % 2) + h // 2, c:c + 2 * HD], zT[:, h, s * P:(s + 1) * P], dfth,
                                   start=True, stop=True)
                mm.then_inc(ab_ps, 1)
            for h in range(NH):
                pe.wait_ge(v_gelu, h + 1)
                pe.wait_ge(ab_stored, 3 + h // 2)
                for n in range(NT):
                    mm = t_.transpose(ps[:, 4 + h, n * P:(n + 1) * P], zT[:, 8 + h, n * P:(n + 1) * P], ident)
                mm.then_inc(vq_ps, 1)
            pe.wait_ge(mixw_landed, 80)
            pe.wait_ge(z_stored, Z_FREE + 28)
            for h in range(NH):
                mm = t_.transpose(ps[:, 0, h * P:(h + 1) * P], ws_raw[:, h, :], ident)
            mm.then_inc(ws_ps, 1)
            pe.wait_ge(ab_stored, NT)
            for h in range(NH):
                if h == 3:
                    pe.wait_ge(ws_stored, 1)
                for c in (0, 1):
                    for s in range(NT):
                        mm = t_.matmul(ps[:, (h + 1) % 4, :], ab[:, s, h, c * HD:(c + 1) * HD], dft[:, c, s, :],
                                       start=(c == 0 and s == 0), stop=(c == 1 and s == NT - 1))
                mm.then_inc(ft_ps, 1)
            for h in range(NH):
                pe.wait_ge(vq_stored, h + 1)
                mm = t_.matmul(ps[:, 4 + h, :].rearrange("p (n q) -> p n q", n=NT), ones[0:1, :],
                               bsp[0:1, h:h + 1, :].to_broadcast([1, NT, P]), start=True, stop=False)
                for n in range(NT):
                    mm = t_.matmul(ps[:, 4 + h, n * P:(n + 1) * P], vq[:, h, n, :], wsT[:, h, :],
                                   start=False, stop=(n == NT - 1))
                mm.then_inc(mix_ps, 1)
            pe.wait_ge(ft_stored, NH)
            for g in range(NH):
                pe.wait_ge(pooled, g + 1)
                t_.matmul(ps[:, g, :], wp[:, g, :], zT[:, 24 + g, :], start=True, stop=True).then_inc(pool_ps, 1)

            def mean_square(nth):
                pe.wait_ge(mix_stored, nth + 1)
                for m in range(NH):
                    pe.wait_ge(sq_ready, 4 * nth + m + 1)
                    mm = t_.matmul(ps[:, 4 + nth, :], mean_w, sq[:, m, :], start=(m == 0), stop=(m == NH - 1))
                mm.then_inc(ms_ps, 1)

            def fourier_out(m):
                pe.wait_ge(pool_stored, m + 1)
                for k in range(NH):
                    mm = t_.matmul(ps[:, m, :], wf[:, k, m * P:(m + 1) * P], fT[:, k, :],
                                   start=(k == 0), stop=(k == NH - 1))
                mm.then_inc(yf_ps, 1)

            mean_square(0)
            fourier_out(0)
            fourier_out(1)
            mean_square(1)
            fourier_out(2)
            fourier_out(3)
            mean_square(2)
            mean_square(3)

            order = [*range(8, 12), *range(12, 16), *range(4, 8), *range(0, 4)]
            with pe.Fori(0, 2) as i:
                for b in (0, 1):
                    pe.wait_ge(w_landed[b], i * 16 + (80 - 16 * b))
                    for t in range(NT):
                        pe.wait_ge(x2_stored, i * 8 + (4 * b + t + 1))
                        if b == 0 and t == 0:
                            pe.wait_ge(yf_stored, NH)
                        for n, k in enumerate(order):
                            if b == 0 and t == 0:
                                pe.wait_ge(y_normed, n + 1)
                            mm = t_.matmul(ps[:, 4 * b + t, :], yT[:, k, t * P:(t + 1) * P], wbuf[b][:, k, :],
                                           start=(n == 0), stop=(n == KT - 1))
                        mm.then_inc(xo_ps, 1)

            pe.wait_ge(router_landed, 64)
            for t in range(NT):
                pe.wait_ge(h2_ready, t + 1)
                for q in range(4):
                    if t == 0:
                        pe.wait_ge(x2_stored, Z_FREE + 9 + q)
                    elif q < 2:
                        pe.wait_ge(h2t_act, 2 * t + q - 1)
                    else:
                        pe.wait_ge(h2t_dve, 2 * t + q - 3)
                    for k in range(4):
                        c = (4 * q + k) * P
                        mm = t_.transpose(ps[:, q, k * P:(k + 1) * P], h2[t % 2][:, c:c + P], ident)
                    mm.then_inc(h2t_ps, 1)
                if t == 0:
                    pe.wait_ge(x2_stored, Z_FREE + 13)
                for k in range(KT):
                    if k == 0:
                        pe.wait_ge(h2t_act, 2 * t + 2)
                    if k == 8:
                        pe.wait_ge(h2t_dve, 2 * t + 2)
                    mm = t_.matmul(ps[:, 4, t * 64:t * 64 + G + E], h2T[:, k, :], wr[:, k, :],
                                   start=(k == 0), stop=(k == KT - 1))
                mm.then_inc(logits_ps, 1)
            pe.wait_ge(routed, 1)
            t_.matmul(ps[:, 5, 0:NT * E], before, A.rearrange("p a b -> p (a b)"), start=True, stop=True)
            t_.matmul(ps[:, 6, 0:NT * E], ones, A.rearrange("p a b -> p (a b)"), start=True, stop=True)\
                .then_inc(counted, 1)

            def plan(e, first=False):
                pe.wait_ge(pick_ready, e + 1)
                if not first:
                    pe.wait_ge(idx_ready, e)
                for j in range(NA):
                    mm = t_.matmul(ps[:, 7, 0:3], pick[:, j, :], asg[:, j // 2, j % 2, 0:3],
                                   start=(j == 0), stop=(j == NA - 1))
                mm.then_inc(plan_ps, 1)

            def transpose_rows(e):
                pe.wait_ge(rows_gathered, e * 16 + 16)
                pe.sem_inc(turns, 1)
                for k in range(KT):
                    c = (k % 8) * SLOTS
                    mm = t_.transpose(ps[:, 2 + k // 8, c:c + SLOTS], hg[0:SLOTS, k * P:(k + 1) * P],
                                      ident[0:SLOTS, 0:SLOTS])
                mm.then_inc(hte_ps, 1)

            def block_products(e):
                plan(e + 1)
                pe.wait_ge(hte_ready, e + 1)
                for q in range(NQ):
                    pe.wait_ge(gu_landed[2 * q], e * 16 + 16)
                    pe.wait_ge(gu_landed[2 * q + 1], e * 16 + 16)
                    for kk in range(QK):
                        k = q * QK + kk
                        for u in (0, 1):
                            for h in (0, 1):
                                mm = t_.matmul(ps[h * SLOTS:(h + 1) * SLOTS, u, 0:HF], hTe[:, k, :],
                                               gu[2 * q + u][:, kk, h * HF:(h + 1) * HF],
                                               start=(k == 0), stop=(k == KT - 1))
                            if kk == QK - 1:
                                mm.then_inc(gu_used[2 * q + u], 1)
                transpose_rows(e + 1)
                pe.wait_ge(act_ready, e + 1)
                for j in range(HF // P):
                    mm = t_.transpose(ps[:, 4, j * P:(j + 1) * P], act[:, j * P:(j + 1) * P], ident)
                mm.then_inc(at_ps, 1)
                pe.wait_ge(at_ready, e + 1)
                for k in range(FT):
                    pe.wait_ge(wd_landed[k % DS], e * 32 + 16 * (k // DS + 1))
                    h, j = divmod(k, HF // P)
                    for n in (0, 1):
                        for c in (0, 1):
                            mm = t_.matmul(ps[c * SLOTS:(c + 1) * SLOTS, 5 + n, :], aT[:, j, h * SLOTS:(h + 1) * SLOTS],
                                           wd[k % DS][:, (2 * c + n) * 512:(2 * c + n + 1) * 512],
                                           start=(k == 0), stop=(k == FT - 1))
                    mm.then_inc(wd_used[k % DS], 1)

            plan(0, first=True)
            transpose_rows(0)
            with pe.Fori(0, E // 2) as i:
                for b in (0, 1):
                    block_products(i * 2 + b)
            n_over = pe.value_load(over_i[0:1, OVER:OVER + 1], min_val=0, max_val=OVER)
            with pe.If(n_over > 0):
                with pe.Fori(E // 2, (E + OVER) // 2) as i:
                    for b in (0, 1):
                        block_products(i * 2 + b)
                pe.wait_ge(at_ready, E + OVER)
            pe.wait_ge(at_ready, E)

        @block.vector
        def _(ve):
            v = nc.vector
            done = 0

            def then(ins):
                nonlocal done
                done += 1
                ins.then_inc(dve_done, 1)
                ve.wait_ge(dve_done, done)

            ve.wait_ge(cols_ps, 1)
            v.tensor_copy(cols, ps[:, 7, 0:NCOL]).then_inc(cols_ready, 1)
            ve.wait_ge(cols_ready, 1)
            def store_ht(t):
                for q in range(4):
                    ve.wait_ge(ht_ps, 4 * t + q + 1)
                    v.tensor_tensor(hT[:, 4 * q:4 * q + 4, t * P:(t + 1) * P],
                                    ps[:, (4 * t + q) % 8, :].rearrange("p (a b) -> p a b", a=4),
                                    cols[:, C_MIX + 4 * q:C_MIX + 4 * q + 4].rearrange("p (a b) -> p a b", b=1)
                                    .to_broadcast([P, 4, P]), ALU.mult).then_inc(ht_stored, 1)

            for t in range(NT):
                ve.wait_ge(x_rms, t + 1)
                v.reciprocal(stat[:, 8 + t:9 + t], stat[:, NT + t:NT + t + 1]).then_inc(x_rinv, 1)
                ve.wait_ge(x_rinv, t + 1)
                v.tensor_scalar(x_sb[:, t, :], x_sb[:, t, :], stat[:, 8 + t:9 + t], None, ALU.mult).then_inc(xn_ready, 1)
                if t:
                    store_ht(t - 1)
            store_ht(NT - 1)

            for s in range(NT):
                ve.wait_ge(ab_ps, s + 1)
                bank = 4 + 2 * (s % 2)
                v.tensor_copy(ab[:, s].rearrange("p (a b) c -> p a (b c)", a=2), ps[:, bank:bank + 2, :])\
                    .then_inc(ab_stored, 1)
            ve.wait_ge(ws_ps, 1)
            v.tensor_copy(wsT.rearrange("p a b -> p (a b)"), ps[:, 0, :]).then_inc(ws_stored, 1)
            ve.wait_ge(z_stored, Z_FREE + 28)
            v.memset(conv_a[:, 0:1], 0.0)
            then(v.memset(conv_a[:, T + 1:T + 2], 0.0))
            for m in range(NH):
                tap = [cols[:, C_CONV + NH * j + m:C_CONV + NH * j + m + 1] for j in range(3)]
                then(v.tensor_tensor(conv_a[:, 1:T + 1], zT[:, 16 + m, :], zT[:, 20 + m, :], ALU.mult))
                then(v.tensor_scalar(conv_t, conv_a[:, 0:T], tap[0], None, ALU.mult))
                for j in (1, 2):
                    then(v.scalar_tensor_tensor(conv_t, conv_a[:, j:T + j], tap[j], conv_t, ALU.mult, ALU.add))
                v.tensor_tensor(yT[:, 8 + m, :], conv_t, zT[:, 12 + m, :], ALU.mult).then_inc(conv_stored, 1)
            v.memset(pool_in[:, 0:PAD], 0.0)
            v.memset(pool_in[:, PAD + T:], 0.0)
            for g, w in enumerate(WINDOWS):
                z = zT[:, 24 + g, :]
                then(v.tensor_copy(pool_in[:, PAD:PAD + T], z))
                src, width = pool_in, 1
                while width < w:
                    dst = pool_a if src is not pool_a else pool_b
                    n = POOLW - 2 * width + 1
                    then(v.tensor_tensor(dst[:, 0:n], src[:, 0:n], src[:, width:width + n], ALU.add))
                    src, width = dst, 2 * width
                o = PAD - w // 2
                then(v.tensor_tensor(src[:, o:o + w // 2], src[:, o:o + w // 2], edges[:, g, 0, 0:w // 2], ALU.mult))
                if w > 2:
                    r = o + T - w // 2 + 1
                    then(v.tensor_tensor(src[:, r:r + w // 2 - 1], src[:, r:r + w // 2 - 1],
                                         edges[:, g, 1, 0:w // 2 - 1], ALU.mult))
                v.scalar_tensor_tensor(z, src[:, o:o + T], 1.0 / w, z, ALU.mult, ALU.subtract).then_inc(pooled, 1)
            for h in range(NH):
                ve.wait_ge(mix_ps, h + 1)
                ve.wait_ge(u_gelu, h + 1)
                v.tensor_tensor(yT[:, 4 + h, :], ps[:, 4 + h, :], zT[:, 4 + h, :], ALU.mult).then_inc(mix_stored, 1)
            for n, (group, stored) in enumerate([(2, conv_stored), (3, pool_stored), (1, mix_stored), (0, yf_stored)]):
                ve.wait_ge(rms_ready, n + 1)
                ve.wait_ge(stored, NH)
                then(v.reciprocal(rstd[:, n, :], rstd[:, n, :]))
                for m in range(NH):
                    c = C_OUT + group * NH + m
                    v.scalar_tensor_tensor(yT[:, group * NH + m, :], yT[:, group * NH + m, :], cols[:, c:c + 1],
                                           rstd[:, n, :], ALU.mult, ALU.mult).then_inc(y_normed, 1)

            ve.sem_inc(x2_stored, Z_FREE)
            ve.wait_ge(x_back, 16)
            with ve.Fori(0, 2) as i:
                for b in (0, 1):
                    for t in range(NT):
                        ve.wait_ge(xo_ps, i * 8 + (4 * b + t + 1))
                        tile = x_sb[:, t, bass.ds(i * 1024 + b * 512, 512)]
                        v.tensor_tensor(tile, ps[:, 4 * b + t, :], tile, ALU.add).then_inc(x2_stored, 1)

            ve.wait_ge(ffn_landed, 16)
            for t in range(NT):
                ve.wait_ge(x2_rms, t + 1)
                v.reciprocal(stat[:, 20 + t:21 + t], stat[:, 16 + t:17 + t]).then_inc(x2_rinv, 1)
                ve.wait_ge(x2_rinv, t + 1)
                if t >= 2:
                    ve.wait_ge(h2_saved[t % 2], 16)
                    ve.wait_ge(h2t_ps, 4 * (t - 1))
                v.scalar_tensor_tensor(h2[t % 2].rearrange("p (k c) -> p c k", k=KT),
                                       x_sb[:, t, :].rearrange("p (c k) -> p c k", k=KT), stat[:, 20 + t:21 + t],
                                       ffn_row.rearrange("p (c k) -> p c k", k=KT), ALU.mult, ALU.mult)\
                    .then_inc(h2_ready, 1)
                for q in (2, 3):
                    ve.wait_ge(h2t_ps, 4 * t + q + 1)
                    if t:
                        ve.wait_ge(logits_ps, t)
                    v.tensor_copy(h2T[:, 4 * q:4 * q + 4, :].rearrange("p a b -> p (a b)"), ps[:, q, :])\
                        .then_inc(h2t_dve, 1)

            def col(n):
                return v4[:, n, :].rearrange("p (a b) -> p a b", b=1)

            def over_last(ap, *shape):
                return ap.to_broadcast([P, *shape])

            ve.wait_ge(logits_ps, NT)
            ve.wait_ge(router_landed, 64)
            ve.wait_ge(consts, 16)
            then(v.tensor_tensor(lg, ps[:, 4, 0:256].rearrange("p (a b) -> p a b", a=NT)[:, :, 0:G + E],
                                 bias36.rearrange("p (a b) -> p a b", a=1).to_broadcast([P, NT, G + E]), ALU.add))
            lgg = lg[:, :, 0:G]
            then(v.tensor_reduce(v4[:, 0, :], lgg, AX.X, ALU.max))
            v.tensor_tensor(lgm, lgg, over_last(col(0), NT, G), ALU.subtract).then_inc(exp_in, 1)
            then(v.tensor_tensor(ohg, lgg, over_last(col(0), NT, G), ALU.is_ge))
            then(v.tensor_tensor(r4, ohg, pri4.rearrange("p (a b) -> p a b", a=1).to_broadcast([P, NT, G]), ALU.mult))
            then(v.tensor_reduce(v4[:, 1, :], r4, AX.X, ALU.max))
            then(v.tensor_tensor(ohg, r4, over_last(col(1), NT, G), ALU.is_equal))
            ohg_b = ohg.rearrange("p a (b c) -> p a b c", c=1).to_broadcast([P, NT, G, EG])
            then(v.tensor_tensor(prod, lg[:, :, G:].rearrange("p a (b c) -> p a b c", b=G), ohg_b, ALU.mult))
            then(v.tensor_reduce(les, prod.rearrange("p a b c -> p a c b"), AX.X, ALU.add))
            pri8_b = pri8.rearrange("p (a b) -> p a b", a=1).to_broadcast([P, NT, EG])
            cur = les
            for k in (0, 1):
                m = 2 + 2 * k
                then(v.tensor_reduce(v4[:, m, :], cur, AX.X, ALU.max))
                then(v.tensor_tensor(r8, cur, over_last(col(m), NT, EG), ALU.is_ge))
                then(v.tensor_tensor(r8, r8, pri8_b, ALU.mult))
                then(v.tensor_reduce(v4[:, m + 1 if k == 0 else 6, :], r8, AX.X, ALU.max))
                then(v.tensor_tensor(oh[:, k], r8, over_last(col(m + 1 if k == 0 else 6), NT, EG), ALU.is_equal))
                if k == 0:
                    then(v.scalar_tensor_tensor(les2, oh[:, 0], -BIG, les, ALU.mult, ALU.add))
                    cur = les2
            v.tensor_tensor(v4[:, 5, :], v4[:, 4, :], v4[:, 2, :], ALU.subtract).then_inc(exp_in, 1)
            for k in (0, 1):
                then(v.tensor_tensor(full[:, k].rearrange("p a (b c) -> p a b c", b=G),
                                     oh[:, k].rearrange("p a (b c) -> p a b c", b=1).to_broadcast([P, NT, G, EG]),
                                     ohg_b, ALU.mult))
            v.tensor_tensor(A, full[:, 0], full[:, 1], ALU.add).then_inc(routed, 1)
            ve.wait_ge(exp_out, 2)
            then(v.tensor_reduce(v4[:, 7, :], lgm, AX.X, ALU.add))
            then(v.tensor_scalar(v4[:, 8, :], v4[:, 5, :], 1.0, None, ALU.add))
            then(v.tensor_tensor(v4[:, 9, :], v4[:, 7, :], v4[:, 8, :], ALU.mult))
            then(v.reciprocal(asg[:, :, 0, 1], v4[:, 9, :]))
            then(v.tensor_tensor(asg[:, :, 1, 1], asg[:, :, 0, 1], v4[:, 5, :], ALU.mult))
            ve.wait_ge(counted, 1)
            then(v.tensor_copy(tot.rearrange("p a b -> p (a b)"), ps[:, 6, 0:NT * E]))
            for t in range(1, NT):
                then(v.tensor_tensor(tot[:, t, :], tot[:, t - 1, :], tot[:, t, :], ALU.add))
            then(v.tensor_copy(Q.rearrange("p a b -> p (a b)"), ps[:, 5, 0:NT * E]))
            then(v.tensor_tensor(Q[:, 1:NT, :], Q[:, 1:NT, :], tot[:, 0:NT - 1, :], ALU.add))
            for b in (0, 1):
                ve.wait_ge(h2_saved[b], 32)
            then(v.tensor_tensor(split_cmp, tot[:, NT - 1, :].rearrange("p (a b) -> p a b", b=1)
                                 .to_broadcast([P, E, NSPLIT]),
                                 thr.rearrange("p (a b) -> p a b", a=1).to_broadcast([P, E, NSPLIT]), ALU.is_gt))
            then(v.tensor_reduce(extra, split_cmp, AX.X, ALU.add))
            then(v.memset(zero32, 0.0))
            then(v.tensor_tensor_scan(over_end, zero32, extra, 0.0, ALU.add, ALU.add))
            then(v.tensor_tensor(id_cmp, over_end.rearrange("p (a b) -> p a b", a=1).to_broadcast([P, OVER, E]),
                                 nums.rearrange("p (a b) -> p a b", b=1).to_broadcast([P, OVER, E]), ALU.is_le))
            then(v.tensor_reduce(over_f[:, 0:OVER], id_cmp, AX.X, ALU.add))
            then(v.tensor_scalar(over_f[:, 0:OVER], over_f[:, 0:OVER], float(E - 1), None, ALU.min))
            then(v.tensor_copy(over_f[:, OVER:], over_end[:, E - 1:E]))
            v.tensor_copy(over_i, over_f).then_inc(counted, 1)
            then(v.tensor_tensor(over_v, over_end, extra, ALU.subtract))
            then(v.tensor_scalar(over_v, over_v, float(SLOTS), float(SLOTS * (E - 1)), ALU.mult, ALU.add))
            then(v.tensor_tensor(over_v, over_v, e64, ALU.subtract))
            then(v.tensor_scalar(t1, Q, float(SLOTS), None, ALU.is_ge))
            then(v.tensor_tensor(t1, t1, over_v.rearrange("p (a b) -> p a b", a=1).to_broadcast([P, NT, E]), ALU.mult))
            then(v.tensor_tensor(Q, Q, t1, ALU.add))
            then(v.tensor_tensor(Q, Q, e64.rearrange("p (a b) -> p a b", a=1).to_broadcast([P, NT, E]), ALU.add))
            for k in (0, 1):
                then(v.tensor_tensor(full[:, k], full[:, k], Q, ALU.mult))
                then(v.tensor_reduce(slot[:, :, k], full[:, k], AX.X, ALU.add))

            def compare():
                v.tensor_tensor(pick, iota64.rearrange("p (a b) -> p a b", a=1).to_broadcast([P, NA, P]),
                                slot.rearrange("p a (b c) -> p (a b) c", c=1).to_broadcast([P, NA, P]),
                                ALU.is_equal).then_inc(pick_ready, 1)

            def next_compare(e):
                v.tensor_scalar(slot, slot, -float(SLOTS), None, ALU.add).then_inc(slots_shifted, 1)
                ve.wait_ge(slots_shifted, e)
                compare()

            def read_plan(e, b):
                ve.wait_ge(plan_ps, e + 1)
                v.tensor_copy(gidx[b], ps[:, 7, 0:1])
                v.tensor_copy(gate[b], ps[:, 7, 1:2])
                v.tensor_scalar(sidx[b], ps[:, 7, 2:3], half, None, ALU.add).then_inc(idx_ready, 1)

            def blocks(i, first=False):
                for b in (0, 1):
                    e = i * 2 + b
                    if b or not first:
                        ve.wait_ge(yg_sent[1 - b], i * 16 + 16 * b)
                    read_plan(e + 1, 1 - b)
                    next_compare(e + 2)
                    ve.wait_ge(gu_used[GUS - 1], e + 1)
                    ve.wait_ge(silu_ready, e + 1)
                    v.tensor_tensor(act, ps[:, 1, 0:HF], sg, ALU.mult).then_inc(act_ready, 1)
                    ve.wait_ge(at_ps, e + 1)
                    v.tensor_copy(aT.rearrange("p a b -> p (a b)"), ps[:, 4, 0:HF]).then_inc(at_ready, 1)

            compare()
            read_plan(0, 0)
            next_compare(1)
            blocks(0, first=True)
            with ve.Fori(1, E // 2) as i:
                blocks(i)
            n_over = ve.value_load(over_i[0:1, OVER:OVER + 1], min_val=0, max_val=OVER)
            with ve.If(n_over > 0):
                with ve.Fori(E // 2, (E + OVER) // 2) as i:
                    blocks(i)
                ve.wait_ge(at_ps, E + OVER)
            ve.wait_ge(at_ps, E)

            ve.wait_ge(final_landed, 16)
            for t in range(NT):
                ve.wait_ge(y_landed[t], 32)
                for k in (0, 1):
                    v.tensor_tensor(x_sb[:, t, :], x_sb[:, t, :], y_rows[t][k], ALU.add).then_inc(summed, 1)
                    ve.wait_ge(summed, 2 * t + k + 1)
                ve.wait_ge(f_rms, t + 1)
                v.reciprocal(stat[:, 8 + t:9 + t], stat[:, NT + t:NT + t + 1]).then_inc(f_rinv, 1)
                ve.wait_ge(f_rinv, t + 1)
                v.scalar_tensor_tensor(x_sb[:, t, :], x_sb[:, t, :], stat[:, 8 + t:9 + t], final_row,
                                       ALU.mult, ALU.mult).then_inc(out_ready, 1)


_INS = ["x", "mix_norm", "w_in", "w_fourier", "w_spatial", "b_spatial", "conv_w", "w_pool", "pool_scale", "out_norm",
        "w_out", "ffn_norm", "w_group", "b_group", "w_router", "b_router", "w_gate", "w_up", "w_down", "final_norm"]


def tables():
    n = np.arange(T)
    seq = 2 * np.pi * (np.outer(n, n) % T) / T
    m = np.arange(HD)
    head = 2 * np.pi * (np.outer(m, m) % HD) / HD
    scale = 1.0 / np.sqrt(T * HD)
    edge = np.ones((NH, 2, PAD))
    for g, w in enumerate(WINDOWS):
        for j in range(w // 2):
            edge[g, 0, j] = w / (j + w // 2)
            edge[g, 1, j] = w / (w - 1 - j)
    return {
        "dft_seq": np.stack([np.cos(seq), np.sin(seq)]).astype(np.float32),
        "dft_head": np.concatenate([np.cos(head) * scale, -np.sin(head) * scale], axis=1).astype(np.float32),
        "edge_scale": np.tile(edge.reshape(1, -1), (P, 1)).astype(np.float32),
    }


def kernel(**inputs):
    import concourse.bacc as bacc
    from concourse.bass_utils import run_bass_kernel_spmd

    nc = bacc.Bacc("TRN2", target_bir_lowering=False, num_devices=1)
    arrays, args = {}, []
    given = {name: np.ascontiguousarray(inputs[name]) for name in _INS}
    for name, a in {**given, **tables()}.items():
        arrays[f"in_{name}"] = a
        args.append(nc.dram_tensor(f"in_{name}", a.shape, mybir.dt.from_np(a.dtype), kind="ExternalInput").ap())
    args.append(nc.dram_tensor("out_0", (1, T, D), F32, kind="ExternalOutput").ap())
    build(nc, *args)
    r = run_bass_kernel_spmd(nc, [arrays], core_ids=[0])
    return r.results[0]["out_0"]
```

```python
from contextlib import ExitStack

import concourse.bass as bass
import numpy as np
from concourse import mybir

F32 = mybir.dt.float32
I32 = mybir.dt.int32
U32 = mybir.dt.uint32
ALU = mybir.AluOpType
ACT = mybir.ActivationFunctionType
AX = mybir.AxisListType

P = 128
T = 512
D = 2048
DG = 512
HD = 128
NH = DG // HD
NT = T // P
KT = D // P
DIN = 7 * DG
NCH = DIN // DG
EPS = 1e-6
WINDOWS = (2, 4, 8, 16)
PAD = 8
POOLW = T + 2 * PAD

G = 4
EG = 8
E = G * EG
DE = 768
HF = DE // 2
FT = DE // P
SLOTS = 64
NSPLIT = T // SLOTS - 1
OVER = 2 * T // SLOTS
NA = 2 * NT
BIG = 1e30

QK = 4
NQ = KT // QK
GUS = 2 * NQ
AHEAD = 2
DS = 4

C_MIX, C_OUT, C_SCALE, C_CONV, NCOL = 0, KT, 2 * KT, 2 * KT + NH, 2 * KT + NH + 3 * NH


def build(nc, x, mix_norm, w_in, w_fourier, w_spatial, b_spatial, conv_w, w_pool, pool_scale, out_norm,
          w_out, ffn_norm, w_group, b_group, w_router, b_router, w_gate, w_up, w_down, final_norm,
          dft_seq, dft_head, edge_scale, out):
    ctx = ExitStack()
    with ctx:
        def sem(name):
            return ctx.enter_context(nc.semaphore(name))

        KB = 256
        arena = ctx.enter_context(nc.sbuf_tensor("arena", [P, 53200], F32))
        ps = ctx.enter_context(nc.psum_tensor("banks", [P, 8, 512], F32))
        h2_dram = nc.dram_tensor("h2_rows", (T, D), F32).ap()

        def at(off, *dims):
            n = int(np.prod(dims))
            v = arena[:, off:off + n]
            if len(dims) == 2:
                v = v.rearrange("p (a b) -> p a b", a=dims[0])
            if len(dims) == 3:
                v = v.rearrange("p (a b c) -> p a b c", a=dims[0], b=dims[1])
            if len(dims) == 4:
                v = v.rearrange("p (a b c d) -> p a b c d", a=dims[0], b=dims[1], c=dims[2])
            return v

        X, H, W0, W1, Z, DFT, CD, SM = (k * KB for k in (0, 32, 64, 96, 128, 184, 200, 201))

        x_sb = at(X, NT, D)
        hT = at(H, KT, T)
        yT = at(H, KT, T)
        wbuf = [at(W0, KT, DG), at(W1, KT, DG)]
        zT = at(Z, NCH * NH, T)
        rows = at(Z + 27 * T, P)
        junk = at(Z, D)
        dft = at(DFT, 2, NT, T)
        dfth = at(CD, 2 * HD)
        wf = at(X, NH, DG)
        ab = at(X + 8 * KB, NT, NH, 2 * HD)
        vq = at(X + 24 * KB, NH, NT, HD)
        fT = at(Z, NH, T)
        rstd = at(Z + 16 * T, NH, T)
        o = W1
        ws_raw = at(o, NH, P)
        wsT = at(o + 512, NH, P)
        wp = at(o + 1024, NH, HD)
        bsp = at(o + 1536, NH, P)
        pool_in = at(o + 2048, POOLW)
        pool_a = at(o + 2048 + POOLW, POOLW)
        pool_b = at(o + 2048 + 2 * POOLW, POOLW)
        o2 = o + 2048 + 3 * POOLW
        conv_a = at(o2, T + 2)
        conv_t = at(o2 + 514, T)
        edges = at(o2 + 514 + T, NH, 2, PAD)
        sq = at(o2 + 514 + T + 64, NH, T)
        assert o2 + 514 + T + 64 + NH * T <= Z

        o = SM
        ident = at(o, P); o += P
        mean_w = at(o, P); o += P
        ones = at(o, P); o += P
        before = at(o, P); o += P
        wr = at(o, KT, G + E); o += KT * (G + E)
        cols = at(o, NCOL); o += NCOL
        bias36 = at(o, G + E); o += G + E
        iota64 = at(o, P); o += P
        stat = at(o, 24); o += 24
        part = at(o, NT, 4); o += 4 * NT
        eps = at(o, 1); o += 1
        pri4 = at(o, G); o += G
        pri8 = at(o, EG); o += EG
        e64 = at(o, E); o += E
        thr = at(o, NSPLIT); o += NSPLIT
        nums = at(o, OVER); o += OVER
        asg = at(o, NT, 2, 2); o += NA * 2
        slot = at(o, NT, 2); o += NA
        gidx = [at(o + k, 1).bitcast(U32) for k in (0, 1)]; o += 2
        held = at(o, 2); o += 2
        held_next = at(o, 2); o += 2
        over_f = at(o, OVER + 1); o += OVER + 1
        over_i = at(o, OVER + 1).bitcast(I32); o += OVER + 1
        assert o <= 53200, o

        ffn_row = at(188 * KB, D)
        h2 = [at(W0, D), at(W0 + 8 * KB, D)]
        h2T = at(W0 + 16 * KB, KT, P)
        gu = [at(Z + s * 12 * KB, QK, DE) for s in range(5)] + [at(H, QK, DE), at(H + 12 * KB, QK, DE),
                                                               at(W0, QK, DE)]
        hg = [at(H + 24 * KB, D), at(188 * KB, D)]
        junk2 = [at(196 * KB, 512), at(198 * KB, 512)]
        pick = at(196 * KB, NA, P)
        yb = at(W0 + 12 * KB, D)
        back = at(W0 + 20 * KB, T)
        tokens = at(W0 + 22 * KB, T)
        hTe = at(W0 + 24 * KB, KT, SLOTS)
        aT = at(W0 + 28 * KB, HF // P, P)
        act = at(W0 + 28 * KB + HF, HF)
        wd = [at(W1 + s * 8 * KB, D) for s in range(DS)]
        final_row = at(H, D)
        junk3 = [at(Z + t * 8 * KB, D) for t in range(NT)]
        o = W1 + 24 * KB
        lg = at(o, NT, G + E); o += NT * (G + E)
        prod = at(o, NT, G, EG); o += NT * E
        both = at(o, NT, 2, E); o += NT * 2 * E
        full = at(o, 2, NT, E); o += 2 * NT * E
        A = at(o, NT, E); o += NT * E
        tot = at(o, NT, E); o += NT * E
        Q = at(o, NT, E); o += NT * E
        t1 = at(o, NT, E); o += NT * E
        les = at(o, NT, EG); o += NT * EG
        les2 = at(o, NT, EG); o += NT * EG
        r8 = at(o, NT, EG); o += NT * EG
        oh = at(o, 2, NT, EG); o += 2 * NT * EG
        ohg = at(o, NT, G); o += NT * G
        lgm = at(o, NT, G); o += NT * G
        r4 = at(o, NT, G); o += NT * G
        v4 = at(o, 12, NT); o += 12 * NT
        extra = at(o, E); o += E
        over_end = at(o, E); o += E
        over_v = at(o, E); o += E
        assert o <= Z, (o, Z)
        split_cmp = at(W0 + 24 * KB, E, NSPLIT)
        id_cmp = at(W0 + 20 * KB, OVER, E)
        zero32 = at(W0 + 28 * KB, E)

        def yb_half(b, c):
            return yb[b * SLOTS:(b + 1) * SLOTS, c * (D // 2):(c + 1) * (D // 2)].rearrange("p (a b) -> p a b", a=2)

        win_v = w_in[0].rearrange("(k p) n -> p k n", p=P)
        wout_v = w_out[0].rearrange("(k p) n -> p k n", p=P)
        wg_v = w_gate[0].rearrange("e (p k) n -> e p k n", k=KT)
        wu_v = w_up[0].rearrange("e (p k) n -> e p k n", k=KT)
        wdn_v = w_down[0].rearrange("e (k p) n -> e p k n", p=P)
        x_v = x[0].rearrange("(t p) n -> p t n", p=P)
        out_v = out[0].rearrange("(t p) n -> p t n", p=P)

        x_landed = [sem(f"x_landed{t}") for t in range(NT)]
        rows_landed = sem("rows_landed")
        dft_landed = sem("dft_landed")
        router_landed = sem("router_landed")
        mixw_landed = sem("mixw_landed")
        w_landed = [sem("w_landed0"), sem("w_landed1")]
        x_back = sem("x_back")
        ffn_landed = sem("ffn_landed")
        final_landed = sem("final_landed")
        gu_landed = [sem(f"gu_landed{s}") for s in range(GUS)]
        wd_landed = [sem(f"wd_landed{s}") for s in range(DS)]
        consts = sem("consts")
        cols_ps, cols_ready = sem("cols_ps"), sem("cols_ready")
        x_sq, x_rms, x_rinv, xn_ready = sem("x_sq"), sem("x_rms"), sem("x_rinv"), sem("xn_ready")
        ht_ps, ht_stored = sem("ht_ps"), sem("ht_stored")
        z_ps, z_stored = sem("z_ps"), sem("z_stored")
        v_gelu, u_gelu = sem("v_gelu"), sem("u_gelu")
        ab_ps, ab_stored = sem("ab_ps"), sem("ab_stored")
        vq_ps, vq_stored = sem("vq_ps"), sem("vq_stored")
        ws_ps, ws_stored = sem("ws_ps"), sem("ws_stored")
        ft_ps, ft_stored = sem("ft_ps"), sem("ft_stored")
        mix_ps, mix_stored = sem("mix_ps"), sem("mix_stored")
        pooled, pool_ps, pool_stored = sem("pooled"), sem("pool_ps"), sem("pool_stored")
        conv_stored = sem("conv_stored")
        yf_ps, yf_stored = sem("yf_ps"), sem("yf_stored")
        sq_ready, ms_ps, rms_ready, y_normed = sem("sq_ready"), sem("ms_ps"), sem("rms_ready"), sem("y_normed")
        xo_ps, x2_stored = sem("xo_ps"), sem("x2_stored")
        x2_sq, x2_sum, x2_rms, x2_rinv = sem("x2_sq"), sem("x2_sum"), sem("x2_rms"), sem("x2_rinv")
        h2_ready = sem("h2_ready")
        h2_saved = [sem("h2_saved0"), sem("h2_saved1")]
        h2t_ps, h2t_act, h2t_dve = sem("h2t_ps"), sem("h2t_act"), sem("h2t_dve")
        logits_ps = sem("logits_ps")
        exp_in, exp_out, routed = sem("exp_in"), sem("exp_out"), sem("routed")
        counted, over_ready = sem("counted"), sem("over_ready")
        pick_ready, plan_ps, plan_read, idx_ready = sem("pick_ready"), sem("plan_ps"), sem("plan_read"), sem("idx_ready")
        slots_shifted = sem("slots_shifted")
        rows_gathered = [sem("rows_gathered0"), sem("rows_gathered1")]
        hte_ps, hte_ready = sem("hte_ps"), sem("hte_ready")
        gu_used = [sem(f"gu_used{s}") for s in range(GUS)]
        silu_ready, act_ready = sem("silu_ready"), sem("act_ready")
        at_ps, at_ready = sem("at_ps"), sem("at_ready")
        wd_used = [sem(f"wd_used{s}") for s in range(DS)]
        tokens_ready, plan_kept = sem("tokens_ready"), sem("plan_kept")
        yb_act, yb_dve, back_ready = sem("yb_act"), sem("yb_dve"), sem("back_ready")
        comb_ps, comb_added = sem("comb_ps"), sem("comb_added")
        f_sq, f_rms, f_rinv, out_ready = sem("f_sq"), sem("f_rms"), sem("f_rinv"), sem("out_ready")
        out_saved = sem("out_saved")
        dve_done = sem("dve_done")
        turns = sem("turns")

        Z_FREE = 8
        OUT_TILES = NT * 4
        MIX_TILES = KT

        block = ctx.enter_context(nc.Block())

        @block.sync
        def _(sp):
            for t in range(NT):
                sp.dma_start(x_sb[:, t, :], x_v[:, t, :]).then_inc(x_landed[t], 16)
            for b in (0, 1):
                sp.dma_start(wbuf[b], win_v[:, :, b * DG:(b + 1) * DG]).then_inc(w_landed[b], 16)
            with sp.Fori(1, 3) as i:
                for b in (0, 1):
                    sp.wait_ge(z_ps, i * 8 + (4 * b - 4))
                    sp.dma_start(wbuf[b], win_v[:, :, bass.ds(i * (2 * DG) + b * DG, DG)]).then_inc(w_landed[b], 16)
            sp.wait_ge(z_ps, 20)
            sp.dma_start(wbuf[0], win_v[:, :, 6 * DG:]).then_inc(w_landed[0], 16)
            sp.wait_ge(ht_ps, 16)
            sp.dma_start(wf, w_fourier[0].rearrange("(k p) n -> p k n", p=P)).then_inc(mixw_landed, 16)
            sp.wait_ge(z_ps, 24)
            sp.dma_start(ws_raw, w_spatial[0].rearrange("h p q -> p h q")).then_inc(mixw_landed, 16)
            sp.dma_start(wp, w_pool[0].rearrange("g c d -> c g d")).then_inc(mixw_landed, 16)
            sp.dma_start(bsp[0:1], b_spatial).then_inc(mixw_landed, 16)
            sp.dma_start(edges.rearrange("p a b c -> p (a b c)"), edge_scale).then_inc(mixw_landed, 16)
            sp.wait_ge(z_ps, 28)
            sp.dma_start(wbuf[0], wout_v[:, :, 0:DG]).then_inc(w_landed[0], 16)
            sp.wait_ge(y_normed, MIX_TILES)
            sp.dma_start(x_sb, x_v).then_inc(x_back, 16)
            sp.dma_start(wbuf[1], wout_v[:, :, DG:2 * DG]).then_inc(w_landed[1], 16)
            sp.dma_start(ffn_row, ffn_norm.to_broadcast([P, D])).then_inc(ffn_landed, 16)

            def gate_up(e, s):
                src = (wg_v, wu_v)[s % 2]
                q = s // 2
                sp.dma_start(gu[s], src[e, :, q * QK:(q + 1) * QK, :]).then_inc(gu_landed[s], 16)

            for s in range(4):
                gate_up(0, s)
            sp.wait_ge(xo_ps, 4)
            sp.dma_start(wbuf[0], wout_v[:, :, 2 * DG:3 * DG]).then_inc(w_landed[0], 16)
            gate_up(0, 4)
            sp.wait_ge(xo_ps, 8)
            sp.dma_start(wbuf[1], wout_v[:, :, 3 * DG:4 * DG]).then_inc(w_landed[1], 16)
            for t in range(NT):
                sp.wait_ge(h2_ready, t + 1)
                sp.dma_start(h2_dram[t * P:(t + 1) * P, :], h2[t % 2]).then_inc(h2_saved[t % 2], 16)
            sp.wait_ge(xo_ps, OUT_TILES)
            gate_up(0, 5)
            gate_up(0, 6)

            def down(expert, k, s):
                sp.dma_start(wd[s], wdn_v[expert, :, k, :]).then_inc(wd_landed[s], 16)

            for k in range(DS - 1):
                down(0, k, k)
            sp.wait_ge(h2t_ps, 16)
            for b in (0, 1):
                sp.wait_ge(h2_saved[b], 32)
            gate_up(0, 7)
            sp.wait_ge(over_ready, 1)
            down(0, DS - 1, DS - 1)

            def next_gate_up(e, expert, s):
                sp.wait_ge(gu_used[s], e)
                sp.sem_inc(turns, 1)
                gate_up(expert, s)

            def next_down(expert, i, b, k):
                c = FT * b + k
                sp.wait_ge(wd_used[c % DS], i * 3 + c // DS)
                sp.sem_inc(turns, 1)
                down(expert, k, c % DS)

            def weights(e, expert, i, b, early=0, ahead=0):
                for s in range(early, GUS):
                    next_gate_up(e, expert, s)
                for k in range(DS):
                    next_down(expert, i, b, k)
                for s in range(ahead):
                    next_gate_up(i * 2 + (b + 1), i * 2 + (b + 1), s)
                for k in range(DS, FT):
                    next_down(expert, i, b, k)

            for s in range(5):
                next_gate_up(1, 1, s)
            for k in range(DS, FT):
                next_down(0, 0, 0, k)
            weights(1, 1, 0, 1, 5, AHEAD)
            with sp.Fori(1, E // 2 - 1) as i:
                for b in (0, 1):
                    weights(i * 2 + b, i * 2 + b, i, b, AHEAD, AHEAD)
            weights(E - 2, E - 2, E // 2 - 1, 0, AHEAD, AHEAD)
            weights(E - 1, E - 1, E // 2 - 1, 1, AHEAD)
            sp.wait_ge(over_ready, 1)
            n_over = sp.value_load(over_i[0:1, OVER:OVER + 1], min_val=0, max_val=OVER)
            with sp.If(n_over > 0):
                with sp.Fori(0, OVER // 2) as j:
                    for b in (0, 1):
                        expert = sp.value_load(over_i[0:1, bass.ds(j * 2 + b, 1)], min_val=0, max_val=E - 1)
                        weights(j * 2 + (E + b), expert, j + E // 2, b)
                sp.wait_ge(gu_used[5], E + OVER)
            sp.wait_ge(gu_used[5], E)
            sp.dma_start(final_row, final_norm.rearrange("(a n) -> a n", a=1).to_broadcast([P, D])).then_inc(final_landed, 16)
            for t in range(NT):
                sp.wait_ge(out_ready, t + 1)
                sp.dma_start(out_v[:, t, :], x_sb[:, t, :]).then_inc(out_saved, 16)
            sp.wait_ge(out_saved, 16 * NT)

        @block.gpsimd
        def _(pool):
            n = 0

            def made(ins):
                nonlocal n
                n += 1
                ins.then_inc(consts, 1)
                pool.wait_ge(consts, n)

            g = nc.gpsimd
            made(g.memset(ident, 0.0))
            made(g.affine_select(out=ident, in_=ident, compare_op=ALU.not_equal, fill=1.0, base=0,
                                 pattern=[[-1, P]], channel_multiplier=1))
            made(g.memset(mean_w, 1.0 / DG))
            made(g.memset(eps, EPS))
            made(g.memset(ones, 1.0))
            made(g.affine_select(out=before, in_=ones, compare_op=ALU.is_gt, fill=0.0, base=0,
                                 pattern=[[1, P]], channel_multiplier=-1))
            made(g.iota(iota64.rearrange("p (a b) -> p a b", a=2), [[0, 2], [1, SLOTS]], 0, 0,
                        allow_small_or_imprecise_dtypes=True))
            made(g.iota(pri4, [[-1, G]], G, 0, allow_small_or_imprecise_dtypes=True))
            made(g.iota(pri8, [[-1, EG]], EG, 0, allow_small_or_imprecise_dtypes=True))
            made(g.iota(e64, [[SLOTS, E]], 0, 0, allow_small_or_imprecise_dtypes=True))
            made(g.iota(thr, [[SLOTS, NSPLIT]], SLOTS, 0, allow_small_or_imprecise_dtypes=True))
            made(g.iota(nums, [[1, OVER]], 0, 0, allow_small_or_imprecise_dtypes=True))
            made(g.iota(asg[:, :, :, 0], [[P, NT], [0, 2]], 0, 1, allow_small_or_imprecise_dtypes=True))
            pool.wait_ge(logits_ps, NT)
            g.iota(tokens, [[1, T]], 0, 0, allow_small_or_imprecise_dtypes=True).then_inc(tokens_ready, 1)

            def gather(e, b, first=False):
                pool.wait_ge(idx_ready, e + 1)
                if not first:
                    pool.wait_ge(hte_ps, e - 1)
                pool.sem_inc(turns, 1)
                g.indirect_dma_start(out=hg[b][0:SLOTS], out_offset=None, in_=h2_dram,
                                     in_offset=bass.IndirectOffsetOnAxis(ap=gidx[b][0:SLOTS], axis=0))\
                    .then_inc(rows_gathered[b], 16)

            for b in (0, 1):
                pool.wait_ge(h2_saved[b], 32)
            gather(0, 0, first=True)
            gather(1, 1, first=True)
            with pool.Fori(0, E // 2) as i:
                for b in (0, 1):
                    gather(i * 2 + (b + 2), b)
            n_over = pool.value_load(over_i[0:1, OVER:OVER + 1], min_val=0, max_val=OVER)
            with pool.If(n_over > 0):
                with pool.Fori(E // 2, (E + OVER) // 2) as i:
                    for b in (0, 1):
                        gather(i * 2 + (b + 2), b)
                for b in (0, 1):
                    pool.wait_ge(rows_gathered[b], 16 * ((E + OVER) // 2 + 1))
            for b in (0, 1):
                pool.wait_ge(rows_gathered[b], 16 * (E // 2 + 1))

        @block.scalar
        def _(ae):
            a = nc.scalar
            ae.dma_start(rows[0:KT], mix_norm[0].rearrange("(r c) -> r c", c=P)).then_inc(rows_landed, 16)
            ae.dma_start(rows[C_OUT:C_OUT + KT], out_norm[0].rearrange("m (r c) -> (m r) c", c=P)).then_inc(rows_landed, 16)
            ae.dma_start(rows[C_SCALE:C_SCALE + NH], pool_scale[0].rearrange("(r c) -> r c", c=P)).then_inc(rows_landed, 16)
            ae.dma_start(rows[C_CONV:NCOL], conv_w[0].rearrange("w (r c) -> (w r) c", c=P)).then_inc(rows_landed, 16)

            ae.wait_ge(consts, 4)
            for t in range(NT):
                ae.wait_ge(x_landed[t], 16)
                if t:
                    ae.wait_ge(x_sq, t)
                a.activation(junk, x_sb[:, t, :], ACT.Square, accum_out=stat[:, t:t + 1]).then_inc(x_sq, 1)
                ae.wait_ge(x_sq, t + 1)
                a.activation(stat[:, NT + t:NT + t + 1], stat[:, t:t + 1], ACT.Sqrt, bias=eps, scale=1.0 / D)\
                    .then_inc(x_rms, 1)
            ae.dma_start(dft, dft_seq.rearrange("c (t p) n -> p c t n", p=P)).then_inc(dft_landed, 16)
            ae.dma_start(dfth, dft_head).then_inc(dft_landed, 16)
            ae.dma_start(wr[:, :, 0:G], w_group[0].rearrange("(p k) n -> p k n", k=KT)).then_inc(router_landed, 16)
            ae.dma_start(wr[:, :, G:], w_router[0].rearrange("(p k) n -> p k n", k=KT)).then_inc(router_landed, 16)
            ae.dma_start(bias36[:, 0:G], b_group.to_broadcast([P, G])).then_inc(router_landed, 16)
            ae.dma_start(bias36[:, G:], b_router.to_broadcast([P, E])).then_inc(router_landed, 16)

            ae.sem_inc(z_stored, Z_FREE)

            def store_z(nth, dst, bank):
                ae.wait_ge(z_ps, nth)
                a.activation(dst, ps[:, bank, :], ACT.Copy).then_inc(z_stored, 1)

            with ae.Fori(0, 3) as i:
                for j in range(8):
                    store_z(i * 8 + (j + 1), zT[:, bass.ds(i * 8 + j, 1), :].rearrange("p a b -> p (a b)"), j)
            for j in range(4):
                store_z(25 + j, zT[:, 24 + j, :], j)

            ae.wait_ge(z_stored, Z_FREE + 28)
            for h in range(NH):
                a.activation(zT[:, 8 + h, :], zT[:, 8 + h, :], ACT.Gelu).then_inc(v_gelu, 1)
            for h in range(NH):
                a.activation(zT[:, 4 + h, :], zT[:, 4 + h, :], ACT.Gelu).then_inc(u_gelu, 1)
            for h in range(NH):
                ae.wait_ge(vq_ps, h + 1)
                a.activation(vq[:, h].rearrange("p n c -> p (n c)"), ps[:, 4 + h, :], ACT.Copy).then_inc(vq_stored, 1)
            for h in range(NH):
                ae.wait_ge(ft_ps, h + 1)
                a.activation(fT[:, h, :], ps[:, (h + 1) % 4, :], ACT.Copy).then_inc(ft_stored, 1)

            def squares(group, done, count):
                ae.wait_ge(done, count)
                if group_order.index(group):
                    ae.wait_ge(ms_ps, group_order.index(group))
                for m in range(NH):
                    a.activation(sq[:, m, :], yT[:, group * NH + m, :], ACT.Square).then_inc(sq_ready, 1)

            group_order = [2, 3, 1, 0]
            def rms(nth):
                ae.wait_ge(ms_ps, nth + 1)
                a.activation(rstd[:, nth, :], ps[:, 4 + nth, :], ACT.Sqrt, bias=eps).then_inc(rms_ready, 1)

            squares(2, conv_stored, 4)
            for g in range(NH):
                ae.wait_ge(pool_ps, g + 1)
                a.activation(yT[:, 12 + g, :], ps[:, g, :], ACT.Copy, scale=cols[:, C_SCALE + g:C_SCALE + g + 1])\
                    .then_inc(pool_stored, 1)
            squares(3, pool_stored, 4)
            for m in (0, 1):
                ae.wait_ge(yf_ps, m + 1)
                a.activation(yT[:, m, :], ps[:, m, :], ACT.Copy).then_inc(yf_stored, 1)
            squares(1, mix_stored, 4)
            rms(0)
            rms(1)
            for m in (2, 3):
                ae.wait_ge(yf_ps, m + 1)
                a.activation(yT[:, m, :], ps[:, m, :], ACT.Copy).then_inc(yf_stored, 1)
            squares(0, yf_stored, 4)
            rms(2)
            rms(3)

            def store_h2t(t):
                for q in (0, 1):
                    ae.wait_ge(h2t_ps, 4 * t + q + 1)
                    if t:
                        ae.wait_ge(logits_ps, t)
                    a.activation(h2T[:, 4 * q:4 * q + 4, :].rearrange("p a b -> p (a b)"), ps[:, 4 + q, :], ACT.Copy)\
                        .then_inc(h2t_act, 1)

            for n in range(4):
                for t in range(NT):
                    j = 4 * n + t
                    ae.wait_ge(x2_stored, j + 1)
                    if j >= 2:
                        ae.wait_ge(x2_sq, j - 1)
                    a.activation(junk2[j % 2], x_sb[:, t, n * 512:(n + 1) * 512], ACT.Square,
                                 accum_out=part[:, t, n:n + 1]).then_inc(x2_sq, 1)
                    if n == 3:
                        ae.wait_ge(x2_sum, t + 1)
                        a.activation(stat[:, 16 + t:17 + t], stat[:, 12 + t:13 + t], ACT.Sqrt, bias=eps, scale=1.0 / D)\
                            .then_inc(x2_rms, 1)
                        if t:
                            store_h2t(t - 1)
            store_h2t(NT - 1)
            ae.wait_ge(exp_in, 1)
            a.activation(lgm, lgm, ACT.Exp).then_inc(exp_out, 1)
            ae.wait_ge(exp_in, 2)
            a.activation(v4[:, 5, :], v4[:, 5, :], ACT.Exp).then_inc(exp_out, 1)

            def store_rows_T(e):
                ae.wait_ge(hte_ps, e + 1)
                a.activation(hTe.rearrange("p (a b) c -> p a (b c)", a=2), ps[:, 2:4, :], ACT.Copy).then_inc(hte_ready, 1)

            def store_down(i, b):
                c = FT * b + FT - 1
                ae.wait_ge(wd_used[c % DS], i * 3 + (c // DS + 1))
                a.activation(yb_half(b, b), ps[b * SLOTS:(b + 1) * SLOTS, 6:8, :], ACT.Copy).then_inc(yb_act, 1)

            def blocks(i, first=False):
                for b in (0, 1):
                    e = i * 2 + b
                    if b:
                        if not first:
                            ae.wait_ge(comb_ps, i * 8)
                        store_down(i, 0)
                    ae.wait_ge(gu_used[GUS - 2], e + 1)
                    a.activation(act, ps[:, 0, 0:HF], ACT.Silu).then_inc(silu_ready, 1)
                    store_rows_T(e + 1)
                store_down(i, 1)

            store_rows_T(0)
            blocks(0, first=True)
            with ae.Fori(1, E // 2) as i:
                blocks(i)
            ae.wait_ge(over_ready, 1)
            n_over = ae.value_load(over_i[0:1, OVER:OVER + 1], min_val=0, max_val=OVER)
            with ae.If(n_over > 0):
                with ae.Fori(E // 2, (E + OVER) // 2) as i:
                    blocks(i)
                ae.wait_ge(comb_added, 4 * (E + OVER))
            ae.wait_ge(comb_added, 4 * E - 6)

            for t in range(NT):
                ae.wait_ge(comb_added, 4 * E - 6 + 2 * t)
                a.activation(junk3[t], x_sb[:, t, :], ACT.Square, accum_out=stat[:, t:t + 1]).then_inc(f_sq, 1)
                ae.wait_ge(f_sq, t + 1)
                a.activation(stat[:, NT + t:NT + t + 1], stat[:, t:t + 1], ACT.Sqrt, bias=eps, scale=1.0 / D)\
                    .then_inc(f_rms, 1)

        @block.tensor
        def _(pe):
            t_ = nc.tensor
            pe.wait_ge(consts, 2)
            pe.wait_ge(rows_landed, 64)
            t_.transpose(ps[:, 7, 0:NCOL], rows[0:NCOL], ident[0:NCOL, 0:NCOL]).then_inc(cols_ps, 1)

            for t in range(NT):
                pe.wait_ge(xn_ready, t + 1)
                for q in range(4):
                    if t >= 2:
                        pe.wait_ge(ht_stored, (t - 2) * 4 + q + 1)
                    elif t == 1 and q == 3:
                        pe.wait_ge(cols_ready, 1)
                    for k in range(4):
                        c = (4 * q + k) * P
                        mm = t_.transpose(ps[:, (4 * t + q) % 8, k * P:(k + 1) * P], x_sb[:, t, c:c + P], ident)
                    mm.then_inc(ht_ps, 1)

            pe.wait_ge(consts, 13)
            pe.wait_ge(ht_stored, 4 * NT)

            def project(w, b, nth):
                pe.wait_ge(w_landed[b], w)
                for m in range(4):
                    pe.wait_ge(z_stored, nth + m)
                    for k in range(KT):
                        mm = t_.matmul(ps[:, 4 * b + m, :], wbuf[b][:, k, m * P:(m + 1) * P], hT[:, k, :],
                                       start=(k == 0), stop=(k == KT - 1))
                    mm.then_inc(z_ps, 1)

            with pe.Fori(0, 3) as i:
                for b in (0, 1):
                    project(i * 16 + 16, b, i * 8 + (4 * b + 1))
            project(64, 0, 25)

            pe.wait_ge(dft_landed, 32)
            for s in range(NT):
                if s < 2:
                    pe.wait_ge(z_stored, Z_FREE + 24)
                else:
                    pe.wait_ge(ab_stored, s - 1)
                for h in range(NH):
                    c = (h % 2) * 2 * HD
                    mm = t_.matmul(ps[:, 4 + 2 * (s % 2) + h // 2, c:c + 2 * HD], zT[:, h, s * P:(s + 1) * P], dfth,
                                   start=True, stop=True)
                mm.then_inc(ab_ps, 1)
            for h in range(NH):
                pe.wait_ge(v_gelu, h + 1)
                pe.wait_ge(ab_stored, 3 + h // 2)
                for n in range(NT):
                    mm = t_.transpose(ps[:, 4 + h, n * P:(n + 1) * P], zT[:, 8 + h, n * P:(n + 1) * P], ident)
                mm.then_inc(vq_ps, 1)
            pe.wait_ge(mixw_landed, 80)
            pe.wait_ge(z_stored, Z_FREE + 28)
            for h in range(NH):
                mm = t_.transpose(ps[:, 0, h * P:(h + 1) * P], ws_raw[:, h, :], ident)
            mm.then_inc(ws_ps, 1)
            pe.wait_ge(ab_stored, NT)
            for h in range(NH):
                if h == 3:
                    pe.wait_ge(ws_stored, 1)
                for c in (0, 1):
                    for s in range(NT):
                        mm = t_.matmul(ps[:, (h + 1) % 4, :], ab[:, s, h, c * HD:(c + 1) * HD], dft[:, c, s, :],
                                       start=(c == 0 and s == 0), stop=(c == 1 and s == NT - 1))
                mm.then_inc(ft_ps, 1)
            for h in range(NH):
                pe.wait_ge(vq_stored, h + 1)
                mm = t_.matmul(ps[:, 4 + h, :].rearrange("p (n q) -> p n q", n=NT), ones[0:1, :],
                               bsp[0:1, h:h + 1, :].to_broadcast([1, NT, P]), start=True, stop=False)
                for n in range(NT):
                    mm = t_.matmul(ps[:, 4 + h, n * P:(n + 1) * P], vq[:, h, n, :], wsT[:, h, :],
                                   start=False, stop=(n == NT - 1))
                mm.then_inc(mix_ps, 1)
            pe.wait_ge(ft_stored, NH)
            for g in range(NH):
                pe.wait_ge(pooled, g + 1)
                t_.matmul(ps[:, g, :], wp[:, g, :], zT[:, 24 + g, :], start=True, stop=True).then_inc(pool_ps, 1)

            def mean_square(nth):
                pe.wait_ge(mix_stored, nth + 1)
                for m in range(NH):
                    pe.wait_ge(sq_ready, 4 * nth + m + 1)
                    mm = t_.matmul(ps[:, 4 + nth, :], mean_w, sq[:, m, :], start=(m == 0), stop=(m == NH - 1))
                mm.then_inc(ms_ps, 1)

            def fourier_out(m):
                pe.wait_ge(pool_stored, m + 1)
                for k in range(NH):
                    mm = t_.matmul(ps[:, m, :], wf[:, k, m * P:(m + 1) * P], fT[:, k, :],
                                   start=(k == 0), stop=(k == NH - 1))
                mm.then_inc(yf_ps, 1)

            mean_square(0)
            fourier_out(0)
            fourier_out(1)
            mean_square(1)
            fourier_out(2)
            fourier_out(3)
            mean_square(2)
            mean_square(3)

            order = [*range(8, 12), *range(12, 16), *range(4, 8), *range(0, 4)]

            def out_tile(n, t):
                j = 4 * n + t
                if j >= 3:
                    pe.wait_ge(x2_stored, j - 2)
                for m, k in enumerate(order):
                    if j == 0:
                        pe.wait_ge(y_normed, m + 1)
                    mm = t_.matmul(ps[:, j % 3, :], yT[:, k, t * P:(t + 1) * P], wbuf[n % 2][:, k, :],
                                   start=(m == 0), stop=(m == KT - 1))
                mm.then_inc(xo_ps, 1)

            def transpose_h2(t):
                pe.wait_ge(h2_ready, t + 1)
                for q in range(4):
                    if t:
                        pe.wait_ge(h2t_act if q < 2 else h2t_dve, 2 * t - 1 + q % 2)
                    for k in range(4):
                        c = (4 * q + k) * P
                        mm = t_.transpose(ps[:, 4 + q, k * P:(k + 1) * P], h2[t % 2][:, c:c + P], ident)
                    mm.then_inc(h2t_ps, 1)

            def router(t):
                for k in range(KT):
                    if k == 0:
                        pe.wait_ge(h2t_act, 2 * t + 2)
                    if k == 8:
                        pe.wait_ge(h2t_dve, 2 * t + 2)
                    mm = t_.matmul(ps[:, 3, t * 64:t * 64 + G + E], h2T[:, k, :], wr[:, k, :],
                                   start=(k == 0), stop=(k == KT - 1))
                mm.then_inc(logits_ps, 1)

            pe.wait_ge(yf_stored, NH)
            for n in range(3):
                pe.wait_ge(w_landed[n % 2], (80, 64, 96)[n])
                for t in range(NT):
                    out_tile(n, t)
            pe.wait_ge(w_landed[1], 80)
            pe.wait_ge(router_landed, 64)
            pe.wait_ge(y_normed, MIX_TILES)
            for t in range(NT):
                out_tile(3, t)
                if t > 1:
                    router(t - 2)
                if t:
                    transpose_h2(t - 1)
            router(NT - 2)
            transpose_h2(NT - 1)
            router(NT - 1)
            pe.wait_ge(routed, 1)
            t_.matmul(ps[:, 0, 0:NT * E], before, A.rearrange("p a b -> p (a b)"), start=True, stop=True)
            t_.matmul(ps[:, 1, 0:NT * E], ones, A.rearrange("p a b -> p (a b)"), start=True, stop=True)\
                .then_inc(counted, 1)

            def plan(e):
                pe.wait_ge(pick_ready, e + 1)
                for j in range(NA):
                    mm = t_.matmul(ps[:, 5, 0:2], pick[:, j, :], asg[:, j // 2, j % 2, :],
                                   start=(j == 0), stop=(j == NA - 1))
                mm.then_inc(plan_ps, 1)

            def transpose_rows(e, i, b):
                pe.wait_ge(rows_gathered[b], i * 16 + 16)
                pe.sem_inc(turns, 1)
                for k in range(KT):
                    c = (k % 8) * SLOTS
                    mm = t_.transpose(ps[:, 2 + k // 8, c:c + SLOTS], hg[b][0:SLOTS, k * P:(k + 1) * P],
                                      ident[0:SLOTS, 0:SLOTS])
                mm.then_inc(hte_ps, 1)

            def combine(pair, t):
                if t == 0:
                    pe.wait_ge(yb_act, pair * 2 + 2)
                    pe.wait_ge(yb_dve, pair * 2 + 2)
                    pe.wait_ge(back_ready, pair + 1)
                for c in (0, 1):
                    if t:
                        pe.wait_ge(comb_added, pair * 8 + (2 * t - 1 + c))
                    for n in (2 * c, 2 * c + 1):
                        mm = t_.matmul(ps[:, 2 + n, :], back[:, t * P:(t + 1) * P], yb[:, n * 512:(n + 1) * 512],
                                       start=True, stop=True)
                    mm.then_inc(comb_ps, 1)

            def block_products(e, i, b, last):
                pe.wait_ge(hte_ready, e + 1)
                for q in range(NQ):
                    pe.wait_ge(gu_landed[2 * q], e * 16 + 16)
                    pe.wait_ge(gu_landed[2 * q + 1], e * 16 + 16)
                    for kk in range(QK):
                        k = q * QK + kk
                        for u in (0, 1):
                            for h in (0, 1):
                                mm = t_.matmul(ps[h * SLOTS:(h + 1) * SLOTS, u, 0:HF], hTe[:, k, :],
                                               gu[2 * q + u][:, kk, h * HF:(h + 1) * HF],
                                               start=(k == 0), stop=(k == KT - 1))
                            if kk == QK - 1:
                                mm.then_inc(gu_used[2 * q + u], 1)
                    if last is not None and q in (1, 2):
                        combine(last, 2 * b + q - 1)
                if last is not None:
                    pe.wait_ge(comb_added, last * 8 + (4 * b + 4))
                plan(e + 2)
                transpose_rows(e + 1, i + b, 1 - b)
                pe.wait_ge(act_ready, e + 1)
                for j in range(HF // P):
                    mm = t_.transpose(ps[:, 4, j * P:(j + 1) * P], act[:, j * P:(j + 1) * P], ident)
                mm.then_inc(at_ps, 1)
                pe.wait_ge(at_ready, e + 1)
                if b:
                    pe.wait_ge(yb_act, i * 2 + 1)
                    pe.wait_ge(yb_dve, i * 2 + 1)
                elif not isinstance(i, int):
                    pe.wait_ge(yb_act, i * 2)
                    pe.wait_ge(yb_dve, i * 2)
                for k in range(FT):
                    c = FT * b + k
                    s = c % DS
                    pe.wait_ge(wd_landed[s], i * 48 + 16 * (c // DS + 1))
                    h, j = divmod(k, HF // P)
                    for n in (0, 1):
                        for c in (0, 1):
                            mm = t_.matmul(ps[c * SLOTS:(c + 1) * SLOTS, 6 + n, :], aT[:, j, h * SLOTS:(h + 1) * SLOTS],
                                           wd[s][:, (2 * c + n) * 512:(2 * c + n + 1) * 512],
                                           start=(k == 0), stop=(k == FT - 1))
                    mm.then_inc(wd_used[s], 1)

            plan(0)
            pe.wait_ge(idx_ready, 1)
            plan(1)
            transpose_rows(0, 0, 0)
            block_products(0, 0, 0, None)
            block_products(1, 0, 1, None)
            with pe.Fori(1, E // 2) as i:
                for b in (0, 1):
                    block_products(i * 2 + b, i, b, i - 1)
            for t in range(NT):
                combine(E // 2 - 1, t)
            n_over = pe.value_load(over_i[0:1, OVER:OVER + 1], min_val=0, max_val=OVER)
            with pe.If(n_over > 0):
                with pe.Fori(E // 2, (E + OVER) // 2) as i:
                    pe.wait_ge(comb_added, i * 8)
                    for b in (0, 1):
                        block_products(i * 2 + b, i, b, None)
                    pe.wait_ge(idx_ready, i * 2 + 4)
                    for t in range(NT):
                        combine(i, t)
                pe.wait_ge(comb_added, 4 * (E + OVER))
            pe.wait_ge(comb_added, 4 * E)

        @block.vector
        def _(ve):
            v = nc.vector
            done = 0

            def then(ins):
                nonlocal done
                done += 1
                ins.then_inc(dve_done, 1)
                ve.wait_ge(dve_done, done)

            ve.wait_ge(cols_ps, 1)
            v.tensor_copy(cols, ps[:, 7, 0:NCOL]).then_inc(cols_ready, 1)
            ve.wait_ge(cols_ready, 1)
            def store_ht(t):
                for q in range(4):
                    ve.wait_ge(ht_ps, 4 * t + q + 1)
                    v.tensor_tensor(hT[:, 4 * q:4 * q + 4, t * P:(t + 1) * P],
                                    ps[:, (4 * t + q) % 8, :].rearrange("p (a b) -> p a b", a=4),
                                    cols[:, C_MIX + 4 * q:C_MIX + 4 * q + 4].rearrange("p (a b) -> p a b", b=1)
                                    .to_broadcast([P, 4, P]), ALU.mult).then_inc(ht_stored, 1)

            for t in range(NT):
                ve.wait_ge(x_rms, t + 1)
                v.reciprocal(stat[:, 8 + t:9 + t], stat[:, NT + t:NT + t + 1]).then_inc(x_rinv, 1)
                ve.wait_ge(x_rinv, t + 1)
                v.tensor_scalar(x_sb[:, t, :], x_sb[:, t, :], stat[:, 8 + t:9 + t], None, ALU.mult).then_inc(xn_ready, 1)
                if t:
                    store_ht(t - 1)
            store_ht(NT - 1)

            for s in range(NT):
                ve.wait_ge(ab_ps, s + 1)
                bank = 4 + 2 * (s % 2)
                v.tensor_copy(ab[:, s].rearrange("p (a b) c -> p a (b c)", a=2), ps[:, bank:bank + 2, :])\
                    .then_inc(ab_stored, 1)
            ve.wait_ge(ws_ps, 1)
            v.tensor_copy(wsT.rearrange("p a b -> p (a b)"), ps[:, 0, :]).then_inc(ws_stored, 1)
            ve.wait_ge(z_stored, Z_FREE + 28)
            v.memset(conv_a[:, 0:1], 0.0)
            then(v.memset(conv_a[:, T + 1:T + 2], 0.0))
            for m in range(NH):
                tap = [cols[:, C_CONV + NH * j + m:C_CONV + NH * j + m + 1] for j in range(3)]
                then(v.tensor_tensor(conv_a[:, 1:T + 1], zT[:, 16 + m, :], zT[:, 20 + m, :], ALU.mult))
                then(v.tensor_scalar(conv_t, conv_a[:, 0:T], tap[0], None, ALU.mult))
                for j in (1, 2):
                    then(v.scalar_tensor_tensor(conv_t, conv_a[:, j:T + j], tap[j], conv_t, ALU.mult, ALU.add))
                v.tensor_tensor(yT[:, 8 + m, :], conv_t, zT[:, 12 + m, :], ALU.mult).then_inc(conv_stored, 1)
            v.memset(pool_in[:, 0:PAD], 0.0)
            v.memset(pool_in[:, PAD + T:], 0.0)
            for g, w in enumerate(WINDOWS):
                z = zT[:, 24 + g, :]
                then(v.tensor_copy(pool_in[:, PAD:PAD + T], z))
                src, width = pool_in, 1
                while width < w:
                    dst = pool_a if src is not pool_a else pool_b
                    n = POOLW - 2 * width + 1
                    then(v.tensor_tensor(dst[:, 0:n], src[:, 0:n], src[:, width:width + n], ALU.add))
                    src, width = dst, 2 * width
                o = PAD - w // 2
                then(v.tensor_tensor(src[:, o:o + w // 2], src[:, o:o + w // 2], edges[:, g, 0, 0:w // 2], ALU.mult))
                if w > 2:
                    r = o + T - w // 2 + 1
                    then(v.tensor_tensor(src[:, r:r + w // 2 - 1], src[:, r:r + w // 2 - 1],
                                         edges[:, g, 1, 0:w // 2 - 1], ALU.mult))
                v.scalar_tensor_tensor(z, src[:, o:o + T], 1.0 / w, z, ALU.mult, ALU.subtract).then_inc(pooled, 1)
            for h in range(NH):
                ve.wait_ge(mix_ps, h + 1)
                ve.wait_ge(u_gelu, h + 1)
                v.tensor_tensor(yT[:, 4 + h, :], ps[:, 4 + h, :], zT[:, 4 + h, :], ALU.mult).then_inc(mix_stored, 1)
            for n, (group, stored) in enumerate([(2, conv_stored), (3, pool_stored), (1, mix_stored), (0, yf_stored)]):
                ve.wait_ge(rms_ready, n + 1)
                ve.wait_ge(stored, NH)
                then(v.reciprocal(rstd[:, n, :], rstd[:, n, :]))
                for m in range(NH):
                    c = C_OUT + group * NH + m
                    v.scalar_tensor_tensor(yT[:, group * NH + m, :], yT[:, group * NH + m, :], cols[:, c:c + 1],
                                           rstd[:, n, :], ALU.mult, ALU.mult).then_inc(y_normed, 1)

            def store_h2t(t):
                for q in (2, 3):
                    ve.wait_ge(h2t_ps, 4 * t + q + 1)
                    if t:
                        ve.wait_ge(logits_ps, t)
                    v.tensor_copy(h2T[:, 4 * q:4 * q + 4, :].rearrange("p a b -> p (a b)"), ps[:, 4 + q, :])\
                        .then_inc(h2t_dve, 1)

            ve.wait_ge(x_back, 16)
            ve.wait_ge(ffn_landed, 16)
            for n in range(4):
                for t in range(NT):
                    j = 4 * n + t
                    ve.wait_ge(xo_ps, j + 1)
                    tile = x_sb[:, t, n * 512:(n + 1) * 512]
                    v.tensor_tensor(tile, ps[:, j % 3, :], tile, ALU.add).then_inc(x2_stored, 1)
                    if n == 3:
                        if t:
                            store_h2t(t - 1)
                        ve.wait_ge(x2_sq, 13 + t)
                        v.tensor_reduce(stat[:, 12 + t:13 + t], part[:, t, :], AX.X, ALU.add).then_inc(x2_sum, 1)
                        ve.wait_ge(x2_rms, t + 1)
                        v.reciprocal(stat[:, 20 + t:21 + t], stat[:, 16 + t:17 + t]).then_inc(x2_rinv, 1)
                        ve.wait_ge(x2_rinv, t + 1)
                        if t >= 2:
                            ve.wait_ge(h2_saved[t % 2], 16)
                            ve.wait_ge(h2t_ps, 4 * (t - 1))
                        v.scalar_tensor_tensor(h2[t % 2].rearrange("p (k c) -> p c k", k=KT),
                                               x_sb[:, t, :].rearrange("p (c k) -> p c k", k=KT), stat[:, 20 + t:21 + t],
                                               ffn_row.rearrange("p (c k) -> p c k", k=KT), ALU.mult, ALU.mult)\
                            .then_inc(h2_ready, 1)
            store_h2t(NT - 1)

            def col(n):
                return v4[:, n, :].rearrange("p (a b) -> p a b", b=1)

            def over_last(ap, *shape):
                return ap.to_broadcast([P, *shape])

            ve.wait_ge(logits_ps, NT)
            ve.wait_ge(router_landed, 64)
            ve.wait_ge(consts, 13)
            then(v.tensor_tensor(lg, ps[:, 3, 0:256].rearrange("p (a b) -> p a b", a=NT)[:, :, 0:G + E],
                                 bias36.rearrange("p (a b) -> p a b", a=1).to_broadcast([P, NT, G + E]), ALU.add))
            lgg = lg[:, :, 0:G]
            then(v.tensor_reduce(v4[:, 0, :], lgg, AX.X, ALU.max))
            v.tensor_tensor(lgm, lgg, over_last(col(0), NT, G), ALU.subtract).then_inc(exp_in, 1)
            then(v.tensor_tensor(ohg, lgg, over_last(col(0), NT, G), ALU.is_ge))
            then(v.tensor_tensor(r4, ohg, pri4.rearrange("p (a b) -> p a b", a=1).to_broadcast([P, NT, G]), ALU.mult))
            then(v.tensor_reduce(v4[:, 1, :], r4, AX.X, ALU.max))
            then(v.tensor_tensor(ohg, r4, over_last(col(1), NT, G), ALU.is_equal))
            ohg_b = ohg.rearrange("p a (b c) -> p a b c", c=1).to_broadcast([P, NT, G, EG])
            then(v.tensor_tensor(prod, lg[:, :, G:].rearrange("p a (b c) -> p a b c", b=G), ohg_b, ALU.mult))
            then(v.tensor_reduce(les, prod.rearrange("p a b c -> p a c b"), AX.X, ALU.add))
            pri8_b = pri8.rearrange("p (a b) -> p a b", a=1).to_broadcast([P, NT, EG])
            cur = les
            for k in (0, 1):
                m = 2 + 2 * k
                then(v.tensor_reduce(v4[:, m, :], cur, AX.X, ALU.max))
                then(v.tensor_tensor(r8, cur, over_last(col(m), NT, EG), ALU.is_ge))
                then(v.tensor_tensor(r8, r8, pri8_b, ALU.mult))
                then(v.tensor_reduce(v4[:, m + 1 if k == 0 else 6, :], r8, AX.X, ALU.max))
                then(v.tensor_tensor(oh[:, k], r8, over_last(col(m + 1 if k == 0 else 6), NT, EG), ALU.is_equal))
                if k == 0:
                    then(v.scalar_tensor_tensor(les2, oh[:, 0], -BIG, les, ALU.mult, ALU.add))
                    cur = les2
            v.tensor_tensor(v4[:, 5, :], v4[:, 4, :], v4[:, 2, :], ALU.subtract).then_inc(exp_in, 1)
            for k in (0, 1):
                then(v.tensor_tensor(full[:, k].rearrange("p a (b c) -> p a b c", b=G),
                                     oh[:, k].rearrange("p a (b c) -> p a b c", b=1).to_broadcast([P, NT, G, EG]),
                                     ohg_b, ALU.mult))
            v.tensor_tensor(A, full[:, 0], full[:, 1], ALU.add).then_inc(routed, 1)
            ve.wait_ge(exp_out, 2)
            then(v.tensor_reduce(v4[:, 7, :], lgm, AX.X, ALU.add))
            then(v.tensor_scalar(v4[:, 8, :], v4[:, 5, :], 1.0, None, ALU.add))
            then(v.tensor_tensor(v4[:, 9, :], v4[:, 7, :], v4[:, 8, :], ALU.mult))
            then(v.reciprocal(asg[:, :, 0, 1], v4[:, 9, :]))
            then(v.tensor_tensor(asg[:, :, 1, 1], asg[:, :, 0, 1], v4[:, 5, :], ALU.mult))
            ve.wait_ge(counted, 1)
            then(v.tensor_copy(tot.rearrange("p a b -> p (a b)"), ps[:, 1, 0:NT * E]))
            for t in range(1, NT):
                then(v.tensor_tensor(tot[:, t, :], tot[:, t - 1, :], tot[:, t, :], ALU.add))
            then(v.tensor_copy(Q.rearrange("p a b -> p (a b)"), ps[:, 0, 0:NT * E]))
            then(v.tensor_tensor(Q[:, 1:NT, :], Q[:, 1:NT, :], tot[:, 0:NT - 1, :], ALU.add))
            then(v.tensor_tensor(split_cmp, tot[:, NT - 1, :].rearrange("p (a b) -> p a b", b=1)
                                 .to_broadcast([P, E, NSPLIT]),
                                 thr.rearrange("p (a b) -> p a b", a=1).to_broadcast([P, E, NSPLIT]), ALU.is_gt))
            then(v.tensor_reduce(extra, split_cmp, AX.X, ALU.add))
            then(v.memset(zero32, 0.0))
            then(v.tensor_tensor_scan(over_end, zero32, extra, 0.0, ALU.add, ALU.add))
            then(v.tensor_tensor(over_v, over_end, extra, ALU.subtract))
            then(v.tensor_scalar(over_v, over_v, float(SLOTS), float(SLOTS * (E - 1)), ALU.mult, ALU.add))
            then(v.tensor_tensor(over_v, over_v, e64, ALU.subtract))
            then(v.tensor_scalar(t1, Q, float(SLOTS), None, ALU.is_ge))
            then(v.tensor_tensor(t1, t1, over_v.rearrange("p (a b) -> p a b", a=1).to_broadcast([P, NT, E]), ALU.mult))
            then(v.tensor_tensor(Q, Q, t1, ALU.add))
            then(v.tensor_tensor(Q, Q, e64.rearrange("p (a b) -> p a b", a=1).to_broadcast([P, NT, E]), ALU.add))
            for k in (0, 1):
                then(v.tensor_tensor(full[:, k], full[:, k], Q, ALU.mult))
                then(v.tensor_reduce(slot[:, :, k], full[:, k], AX.X, ALU.add))

            def compare():
                v.tensor_tensor(pick, iota64.rearrange("p (a b) -> p a b", a=1).to_broadcast([P, NA, P]),
                                slot.rearrange("p a (b c) -> p (a b) c", c=1).to_broadcast([P, NA, P]),
                                ALU.is_equal).then_inc(pick_ready, 1)

            def next_compare(e):
                v.tensor_scalar(slot, slot, -float(SLOTS), None, ALU.add).then_inc(slots_shifted, 1)
                ve.wait_ge(slots_shifted, e)
                compare()

            def read_plan(e, b):
                ve.wait_ge(plan_ps, e + 1)
                r = slice(b * SLOTS, (b + 1) * SLOTS)
                v.tensor_copy(held_next[r], ps[r, 5, 0:2])
                v.tensor_copy(gidx[b], ps[:, 5, 0:1]).then_inc(idx_ready, 1)

            def keep_plan(pair):
                ve.wait_ge(idx_ready, pair * 2 + 2)
                v.tensor_copy(held, held_next).then_inc(plan_kept, 1)

            def add_rows(pair, t):
                for c in (0, 1):
                    ve.wait_ge(comb_ps, pair * 8 + (2 * t + c + 1))
                    tile = x_sb[:, t, c * 1024:(c + 1) * 1024].rearrange("p (a b) -> p a b", a=2)
                    v.tensor_tensor(tile, ps[:, 2 + 2 * c:4 + 2 * c, :], tile, ALU.add).then_inc(comb_added, 1)

            def store_down(i, b):
                c = FT * b + FT - 1
                ve.wait_ge(wd_used[c % DS], i * 3 + (c // DS + 1))
                h = 1 - b
                v.tensor_copy(yb_half(b, h), ps[h * SLOTS:(h + 1) * SLOTS, 6:8, :]).then_inc(yb_dve, 1)

            def block_steps(e, i, b, last):
                if last is not None:
                    add_rows(last, 2 * b)
                    add_rows(last, 2 * b + 1)
                if b:
                    ve.wait_ge(plan_kept, i + 1)
                    v.tensor_scalar(back, tokens, held[:, 0:1], held[:, 1:2], ALU.is_equal, ALU.mult)\
                        .then_inc(back_ready, 1)
                    store_down(i, 0)
                ve.wait_ge(gu_used[GUS - 1], e + 1)
                ve.wait_ge(silu_ready, e + 1)
                v.tensor_tensor(act, ps[:, 1, 0:HF], act, ALU.mult).then_inc(act_ready, 1)
                if not b:
                    ve.wait_ge(plan_kept, i + 1)
                read_plan(e + 2, b)
                ve.wait_ge(at_ps, e + 1)
                v.tensor_copy(aT.rearrange("p a b -> p (a b)"), ps[:, 4, 0:HF]).then_inc(at_ready, 1)
                next_compare(e + 3)
                if b:
                    ve.wait_ge(back_ready, i + 1)
                    keep_plan(i + 1)
                    store_down(i, 1)

            compare()
            read_plan(0, 0)
            next_compare(1)
            read_plan(1, 1)
            next_compare(2)
            then(v.tensor_tensor(id_cmp, over_end.rearrange("p (a b) -> p a b", a=1).to_broadcast([P, OVER, E]),
                                 nums.rearrange("p (a b) -> p a b", b=1).to_broadcast([P, OVER, E]), ALU.is_le))
            then(v.tensor_reduce(over_f[:, 0:OVER], id_cmp, AX.X, ALU.add))
            then(v.tensor_scalar(over_f[:, 0:OVER], over_f[:, 0:OVER], float(E - 1), None, ALU.min))
            then(v.tensor_copy(over_f[:, OVER:], over_end[:, E - 1:E]))
            v.tensor_copy(over_i, over_f).then_inc(over_ready, 1)
            ve.wait_ge(tokens_ready, 1)
            keep_plan(0)
            block_steps(0, 0, 0, None)
            block_steps(1, 0, 1, None)
            with ve.Fori(1, E // 2) as i:
                for b in (0, 1):
                    block_steps(i * 2 + b, i, b, i - 1)
            for t in range(NT):
                add_rows(E // 2 - 1, t)
            n_over = ve.value_load(over_i[0:1, OVER:OVER + 1], min_val=0, max_val=OVER)
            with ve.If(n_over > 0):
                with ve.Fori(E // 2, (E + OVER) // 2) as i:
                    for b in (0, 1):
                        block_steps(i * 2 + b, i, b, None)
                    for t in range(NT):
                        add_rows(i, t)
                ve.wait_ge(comb_added, 4 * (E + OVER))
            ve.wait_ge(comb_added, 4 * E)

            ve.wait_ge(final_landed, 16)
            for t in range(NT):
                ve.wait_ge(f_rms, t + 1)
                v.reciprocal(stat[:, 8 + t:9 + t], stat[:, NT + t:NT + t + 1]).then_inc(f_rinv, 1)
                ve.wait_ge(f_rinv, t + 1)
                v.scalar_tensor_tensor(x_sb[:, t, :], x_sb[:, t, :], stat[:, 8 + t:9 + t], final_row,
                                       ALU.mult, ALU.mult).then_inc(out_ready, 1)


_INS = ["x", "mix_norm", "w_in", "w_fourier", "w_spatial", "b_spatial", "conv_w", "w_pool", "pool_scale", "out_norm",
        "w_out", "ffn_norm", "w_group", "b_group", "w_router", "b_router", "w_gate", "w_up", "w_down", "final_norm"]


def tables():
    n = np.arange(T)
    seq = 2 * np.pi * (np.outer(n, n) % T) / T
    m = np.arange(HD)
    head = 2 * np.pi * (np.outer(m, m) % HD) / HD
    scale = 1.0 / np.sqrt(T * HD)
    edge = np.ones((NH, 2, PAD))
    for g, w in enumerate(WINDOWS):
        for j in range(w // 2):
            edge[g, 0, j] = w / (j + w // 2)
            edge[g, 1, j] = w / (w - 1 - j)
    return {
        "dft_seq": np.stack([np.cos(seq), np.sin(seq)]).astype(np.float32),
        "dft_head": np.concatenate([np.cos(head) * scale, -np.sin(head) * scale], axis=1).astype(np.float32),
        "edge_scale": np.tile(edge.reshape(1, -1), (P, 1)).astype(np.float32),
    }


def kernel(**inputs):
    import concourse.bacc as bacc
    from concourse.bass_utils import run_bass_kernel_spmd

    nc = bacc.Bacc("TRN2", target_bir_lowering=False, num_devices=1)
    arrays, args = {}, []
    given = {name: np.ascontiguousarray(inputs[name]) for name in _INS}
    for name, a in {**given, **tables()}.items():
        arrays[f"in_{name}"] = a
        args.append(nc.dram_tensor(f"in_{name}", a.shape, mybir.dt.from_np(a.dtype), kind="ExternalInput").ap())
    args.append(nc.dram_tensor("out_0", (1, T, D), F32, kind="ExternalOutput").ap())
    build(nc, *args)
    r = run_bass_kernel_spmd(nc, [arrays], core_ids=[0])
    return r.results[0]["out_0"]
```

```python
from contextlib import ExitStack

import concourse.bass as bass
import numpy as np
from concourse import mybir

F32 = mybir.dt.float32
F32R = mybir.dt.float32r
I32 = mybir.dt.int32
U32 = mybir.dt.uint32
ALU = mybir.AluOpType
ACT = mybir.ActivationFunctionType
AX = mybir.AxisListType

P = 128
T = 512
D = 2048
DG = 512
HD = 128
NH = DG // HD
NT = T // P
KT = D // P
DIN = 7 * DG
NCH = DIN // DG
EPS = 1e-6
WINDOWS = (2, 4, 8, 16)
PAD = 8
POOLW = T + 2 * PAD

G = 4
EG = 8
E = G * EG
DE = 768
HF = DE // 2
FT = DE // P
SLOTS = 64
NSPLIT = T // SLOTS - 1
OVER = 2 * T // SLOTS
NA = 2 * NT
BIG = 1e30
UK = 4
NU = KT // UK
UNITS = NCH * NU

QK = 4
NQ = KT // QK
GUS = 2 * NQ
AHEAD = 2
DS = 4

C_MIX, C_OUT, C_SCALE, C_CONV, NCOL = 0, KT, 2 * KT, 2 * KT + NH, 2 * KT + NH + 3 * NH


def build(nc, x, mix_norm, w_in, w_fourier, w_spatial, b_spatial, conv_w, w_pool, pool_scale, out_norm,
          w_out, ffn_norm, w_group, b_group, w_router, b_router, w_gate, w_up, w_down, final_norm,
          dft_seq, dft_head, edge_scale, out):
    ctx = ExitStack()
    with ctx:
        def sem(name):
            return ctx.enter_context(nc.semaphore(name))

        KB = 256
        R = 32 * KB
        with ExitStack() as first:
            split_x, split_h, _, split_w1 = [first.enter_context(nc.sbuf_tensor(f"split_{name}", [P, R], F32R))
                                             for name in ("x", "h", "w0", "w1")]
        regions = [ctx.enter_context(nc.sbuf_tensor(f"region_{name}", [P, n], F32))
                   for name, n in (("x", R), ("h", R), ("w0", R), ("w1", R), ("rest", 53200 - 4 * R))]
        ps = ctx.enter_context(nc.psum_tensor("banks", [P, 8, 512], F32))
        h2_dram = nc.dram_tensor("h2_rows", (T, D), F32).ap()

        def at(off, *dims):
            n = int(np.prod(dims))
            r = min(off // R, 4)
            off -= r * R
            v = regions[r][:, off:off + n]
            if len(dims) == 2:
                v = v.rearrange("p (a b) -> p a b", a=dims[0])
            if len(dims) == 3:
                v = v.rearrange("p (a b c) -> p a b c", a=dims[0], b=dims[1])
            if len(dims) == 4:
                v = v.rearrange("p (a b c d) -> p a b c d", a=dims[0], b=dims[1], c=dims[2])
            return v

        X, H, W0, W1, Z, DFT, CD, SM = (k * KB for k in (0, 32, 64, 96, 128, 184, 200, 201))

        x_sb = at(X, NT, D)
        h_hi = split_h[:, 0:KT * T].rearrange("p (a b) -> p a b", a=KT)
        h_full = at(W1, KT, T)
        h_lo = split_w1[:, 0:KT * T].rearrange("p (a b) -> p a b", a=KT)
        w_raw = [at(W0 + s * 8 * KB, UK, DG) for s in range(NU)]
        w_hi, w_lo = ([split_x[:, o:o + UK * DG].rearrange("p (a b) -> p a b", a=UK) for o in (c, c + 16 * KB)]
                      for c in (0, 8 * KB))
        yT = at(H, KT, T)
        wbuf = [at(W0, KT, DG), at(W1, KT, DG)]
        zT = at(Z, NCH * NH, T)
        rows = at(Z + 27 * T, P)
        junk = at(Z, D)
        diag = at(Z + 20 * T, NT, P)
        dft = at(DFT, 2, NT, T)
        dfth = at(CD, 2 * HD)
        wf = at(X, NH, DG)
        ab = at(X + 8 * KB, NT, NH, 2 * HD)
        vq = at(X + 24 * KB, NH, NT, HD)
        fT = at(Z, NH, T)
        rstd = at(Z + 16 * T, NH, T)
        o = W1
        ws_raw = at(o, NH, P)
        wsT = at(o + 512, NH, P)
        wp = at(o + 1024, NH, HD)
        bsp = at(o + 1536, NH, P)
        pool_in = at(o + 2048, POOLW)
        pool_a = at(o + 2048 + POOLW, POOLW)
        pool_b = at(o + 2048 + 2 * POOLW, POOLW)
        o2 = o + 2048 + 3 * POOLW
        conv_a = at(o2, T + 2)
        conv_t = at(o2 + 514, T)
        edges = at(o2 + 514 + T, NH, 2, PAD)
        sq = at(o2 + 514 + T + 64, NH, T)
        assert o2 + 514 + T + 64 + NH * T <= Z

        o = SM
        ident = at(o, P); o += P
        mean_w = at(o, P); o += P
        ones = at(o, P); o += P
        before = at(o, P); o += P
        rstd_x = at(o, T)
        wr = at(o, KT, G + E); o += KT * (G + E)
        cols = at(o, NCOL); o += NCOL
        bias36 = at(o, G + E); o += G + E
        iota64 = at(o, P); o += P
        stat = at(o, 24); o += 24
        part = at(o, NT, 4); o += 4 * NT
        eps = at(o, 1); o += 1
        pri4 = at(o, G); o += G
        pri8 = at(o, EG); o += EG
        e64 = at(o, E); o += E
        thr = at(o, NSPLIT); o += NSPLIT
        nums = at(o, OVER); o += OVER
        asg = at(o, NT, 2, 2); o += NA * 2
        slot = at(o, NT, 2); o += NA
        gidx = [at(o + k, 1).bitcast(U32) for k in (0, 1)]; o += 2
        held = at(o, 2); o += 2
        held_next = at(o, 2); o += 2
        over_f = at(o, OVER + 1); o += OVER + 1
        over_i = at(o, OVER + 1).bitcast(I32); o += OVER + 1
        assert o <= 53200, o

        ffn_row = at(188 * KB, D)
        h2 = [at(W0, D), at(W0 + 8 * KB, D)]
        h2T = at(W0 + 16 * KB, KT, P)
        gu = [at(Z + s * 12 * KB, QK, DE) for s in range(5)] + [at(H, QK, DE), at(H + 12 * KB, QK, DE),
                                                               at(W0, QK, DE)]
        hg = [at(H + 24 * KB, D), at(188 * KB, D)]
        junk2 = [at(196 * KB, 512), at(198 * KB, 512)]
        pick = at(196 * KB, NA, P)
        yb = at(W0 + 12 * KB, D)
        back = at(W0 + 20 * KB, T)
        tokens = at(W0 + 22 * KB, T)
        hTe = at(W0 + 24 * KB, KT, SLOTS)
        aT = at(W0 + 28 * KB, HF // P, P)
        act = at(W0 + 28 * KB + HF, HF)
        wd = [at(W1 + s * 8 * KB, D) for s in range(DS)]
        final_row = at(H, D)
        junk3 = [at(Z + t * 8 * KB, D) for t in range(NT)]
        o = W1 + 24 * KB
        lg = at(o, NT, G + E); o += NT * (G + E)
        prod = at(o, NT, G, EG); o += NT * E
        both = at(o, NT, 2, E); o += NT * 2 * E
        full = at(o, 2, NT, E); o += 2 * NT * E
        A = at(o, NT, E); o += NT * E
        tot = at(o, NT, E); o += NT * E
        Q = at(o, NT, E); o += NT * E
        t1 = at(o, NT, E); o += NT * E
        les = at(o, NT, EG); o += NT * EG
        les2 = at(o, NT, EG); o += NT * EG
        r8 = at(o, NT, EG); o += NT * EG
        oh = at(o, 2, NT, EG); o += 2 * NT * EG
        ohg = at(o, NT, G); o += NT * G
        lgm = at(o, NT, G); o += NT * G
        r4 = at(o, NT, G); o += NT * G
        v4 = at(o, 12, NT); o += 12 * NT
        extra = at(o, E); o += E
        over_end = at(o, E); o += E
        over_v = at(o, E); o += E
        assert o <= Z, (o, Z)
        split_cmp = at(W0 + 24 * KB, E, NSPLIT)
        id_cmp = at(W0 + 20 * KB, OVER, E)
        zero32 = at(W0 + 28 * KB, E)

        def yb_half(b, c):
            return yb[b * SLOTS:(b + 1) * SLOTS, c * (D // 2):(c + 1) * (D // 2)].rearrange("p (a b) -> p a b", a=2)

        win_v = w_in[0].rearrange("(k p) n -> p k n", p=P)
        wout_v = w_out[0].rearrange("(k p) n -> p k n", p=P)
        wg_v = w_gate[0].rearrange("e (p k) n -> e p k n", k=KT)
        wu_v = w_up[0].rearrange("e (p k) n -> e p k n", k=KT)
        wdn_v = w_down[0].rearrange("e (k p) n -> e p k n", p=P)
        x_v = x[0].rearrange("(t p) n -> p t n", p=P)
        out_v = out[0].rearrange("(t p) n -> p t n", p=P)

        x_landed = [sem(f"x_landed{t}") for t in range(NT)]
        rows_landed = sem("rows_landed")
        dft_landed = sem("dft_landed")
        router_landed = sem("router_landed")
        mixw_landed = sem("mixw_landed")
        w_landed = [sem(f"w_landed{q}") for q in range(NU)]
        wout_landed = [sem("wout_landed0"), sem("wout_landed1")]
        x_back = sem("x_back")
        ffn_landed = sem("ffn_landed")
        final_landed = sem("final_landed")
        gu_landed = [sem(f"gu_landed{s}") for s in range(GUS)]
        wd_landed = [sem(f"wd_landed{s}") for s in range(DS)]
        consts = sem("consts")
        cols_ps, cols_ready = sem("cols_ps"), sem("cols_ready")
        x_sq, x_rms, x_rinv = sem("x_sq"), sem("x_rms"), sem("x_rinv")
        diag_ready, rstd_ps = sem("diag_ready"), sem("rstd_ps")
        ht_ps, ht_full, ht_hi, ht_lo_dve, ht_lo_pool = (sem("ht_ps"), sem("ht_full"), sem("ht_hi"), sem("ht_lo_dve"),
                                                        sem("ht_lo_pool"))
        w_scaled, w_hi_ready, w_ready, w_used = sem("w_scaled"), sem("w_hi_ready"), sem("w_ready"), sem("w_used")
        z_ps, z_stored = sem("z_ps"), sem("z_stored")
        v_gelu, u_gelu = sem("v_gelu"), sem("u_gelu")
        ab_ps, ab_stored = sem("ab_ps"), sem("ab_stored")
        vq_ps, vq_stored = sem("vq_ps"), sem("vq_stored")
        ws_ps, ws_stored = sem("ws_ps"), sem("ws_stored")
        ft_ps, ft_stored = sem("ft_ps"), sem("ft_stored")
        mix_ps, mix_stored = sem("mix_ps"), sem("mix_stored")
        pooled, pool_ps, pool_stored = sem("pooled"), sem("pool_ps"), sem("pool_stored")
        conv_stored = sem("conv_stored")
        yf_ps, yf_stored = sem("yf_ps"), sem("yf_stored")
        sq_summed = sem("sq_summed")
        sq_ready, ms_ps, rms_ready, y_normed = sem("sq_ready"), sem("ms_ps"), sem("rms_ready"), sem("y_normed")
        xo_ps, x2_stored = sem("xo_ps"), sem("x2_stored")
        x2_sq, x2_sum, x2_rms, x2_rinv = sem("x2_sq"), sem("x2_sum"), sem("x2_rms"), sem("x2_rinv")
        h2_ready = sem("h2_ready")
        h2_saved = [sem("h2_saved0"), sem("h2_saved1")]
        h2t_ps, h2t_act, h2t_dve = sem("h2t_ps"), sem("h2t_act"), sem("h2t_dve")
        logits_ps = sem("logits_ps")
        exp_in, exp_out, routed = sem("exp_in"), sem("exp_out"), sem("routed")
        counted, over_ready = sem("counted"), sem("over_ready")
        pick_ready, plan_ps, idx_ready = sem("pick_ready"), sem("plan_ps"), sem("idx_ready")
        slots_shifted = sem("slots_shifted")
        rows_gathered = [sem("rows_gathered0"), sem("rows_gathered1")]
        hte_ps, hte_ready = sem("hte_ps"), sem("hte_ready")
        gu_used = [sem(f"gu_used{s}") for s in range(GUS)]
        silu_ready, act_ready = sem("silu_ready"), sem("act_ready")
        at_ps, at_ready = sem("at_ps"), sem("at_ready")
        wd_used = [sem(f"wd_used{s}") for s in range(DS)]
        tokens_ready, plan_kept = sem("tokens_ready"), sem("plan_kept")
        yb_act, yb_dve, back_ready = sem("yb_act"), sem("yb_dve"), sem("back_ready")
        comb_ps, comb_added = sem("comb_ps"), sem("comb_added")
        f_sq, f_rms, f_rinv, out_ready = sem("f_sq"), sem("f_rms"), sem("f_rinv"), sem("out_ready")
        out_saved = sem("out_saved")
        dve_done = sem("dve_done")
        turns = sem("turns")

        Z_FREE = 8
        OUT_TILES = NT * 4
        MIX_TILES = KT

        block = ctx.enter_context(nc.Block())

        @block.sync
        def _(sp):
            def rows_in(dst, src):
                sp.dma_start(dst, src).then_inc(rows_landed, 16)

            def w_in_unit(chunk, q):
                sp.dma_start(w_raw[q], win_v[:, q * UK:(q + 1) * UK, chunk]).then_inc(w_landed[q], 16)

            for t in range(NT):
                sp.dma_start(x_sb[:, t, :], x_v[:, t, :]).then_inc(x_landed[t], 16)
                if t == 0:
                    rows_in(rows[0:KT], mix_norm[0].rearrange("(r c) -> r c", c=P))
                    rows_in(rows[C_OUT:C_OUT + KT], out_norm[0].rearrange("m (r c) -> (m r) c", c=P))
                    rows_in(rows[C_SCALE:C_SCALE + NH], pool_scale[0].rearrange("(r c) -> r c", c=P))
                    rows_in(rows[C_CONV:NCOL], conv_w[0].rearrange("w (r c) -> (w r) c", c=P))
            for q in range(NU):
                w_in_unit(slice(0, DG), q)
            with sp.Fori(1, NCH) as i:
                for q in range(NU):
                    sp.wait_ge(w_ready, i * NU + (q + 1 - NU))
                    w_in_unit(bass.ds(i * DG, DG), q)
            sp.wait_ge(w_ready, UNITS)
            sp.dma_start(wbuf[0], wout_v[:, :, 0:DG]).then_inc(wout_landed[0], 16)
            sp.wait_ge(z_ps, 4 * NCH)
            sp.dma_start(ws_raw, w_spatial[0].rearrange("h p q -> p h q")).then_inc(mixw_landed, 16)
            sp.dma_start(bsp[0:1], b_spatial).then_inc(mixw_landed, 16)
            sp.dma_start(edges.rearrange("p a b c -> p (a b c)"), edge_scale).then_inc(mixw_landed, 16)
            sp.dma_start(wp, w_pool[0].rearrange("g c d -> c g d")).then_inc(mixw_landed, 16)
            sp.dma_start(wf, w_fourier[0].rearrange("(k p) n -> p k n", p=P)).then_inc(mixw_landed, 16)
            sp.wait_ge(y_normed, MIX_TILES)
            sp.dma_start(x_sb, x_v).then_inc(x_back, 16)
            sp.dma_start(wbuf[1], wout_v[:, :, DG:2 * DG]).then_inc(wout_landed[1], 16)
            sp.dma_start(ffn_row, ffn_norm.to_broadcast([P, D])).then_inc(ffn_landed, 16)

            def gate_up(e, s):
                src = (wg_v, wu_v)[s % 2]
                q = s // 2
                sp.dma_start(gu[s], src[e, :, q * QK:(q + 1) * QK, :]).then_inc(gu_landed[s], 16)

            for s in range(4):
                gate_up(0, s)
            sp.wait_ge(xo_ps, 4)
            sp.dma_start(wbuf[0], wout_v[:, :, 2 * DG:3 * DG]).then_inc(wout_landed[0], 16)
            gate_up(0, 4)
            sp.wait_ge(xo_ps, 8)
            sp.dma_start(wbuf[1], wout_v[:, :, 3 * DG:4 * DG]).then_inc(wout_landed[1], 16)
            for t in range(NT):
                sp.wait_ge(h2_ready, t + 1)
                sp.dma_start(h2_dram[t * P:(t + 1) * P, :], h2[t % 2]).then_inc(h2_saved[t % 2], 16)
            sp.wait_ge(xo_ps, OUT_TILES)
            gate_up(0, 5)
            gate_up(0, 6)

            def down(expert, k, s):
                sp.dma_start(wd[s], wdn_v[expert, :, k, :]).then_inc(wd_landed[s], 16)

            for k in range(DS - 1):
                down(0, k, k)
            sp.wait_ge(h2t_ps, 16)
            for b in (0, 1):
                sp.wait_ge(h2_saved[b], 32)
            gate_up(0, 7)
            sp.wait_ge(over_ready, 1)
            down(0, DS - 1, DS - 1)

            def next_gate_up(e, expert, s):
                sp.wait_ge(gu_used[s], e)
                sp.sem_inc(turns, 1)
                gate_up(expert, s)

            def next_down(expert, i, b, k):
                c = FT * b + k
                sp.wait_ge(wd_used[c % DS], i * 3 + c // DS)
                sp.sem_inc(turns, 1)
                down(expert, k, c % DS)

            def weights(e, expert, i, b, early=0, ahead=0):
                for s in range(early, GUS):
                    next_gate_up(e, expert, s)
                for k in range(DS):
                    next_down(expert, i, b, k)
                for s in range(ahead):
                    next_gate_up(i * 2 + (b + 1), i * 2 + (b + 1), s)
                for k in range(DS, FT):
                    next_down(expert, i, b, k)

            for s in range(5):
                next_gate_up(1, 1, s)
            for k in range(DS, FT):
                next_down(0, 0, 0, k)
            weights(1, 1, 0, 1, 5, AHEAD)
            with sp.Fori(1, E // 2 - 1) as i:
                for b in (0, 1):
                    weights(i * 2 + b, i * 2 + b, i, b, AHEAD, AHEAD)
            weights(E - 2, E - 2, E // 2 - 1, 0, AHEAD, AHEAD)
            weights(E - 1, E - 1, E // 2 - 1, 1, AHEAD)
            sp.wait_ge(over_ready, 1)
            n_over = sp.value_load(over_i[0:1, OVER:OVER + 1], min_val=0, max_val=OVER)
            with sp.If(n_over > 0):
                with sp.Fori(0, OVER // 2) as j:
                    for b in (0, 1):
                        expert = sp.value_load(over_i[0:1, bass.ds(j * 2 + b, 1)], min_val=0, max_val=E - 1)
                        weights(j * 2 + (E + b), expert, j + E // 2, b)
                sp.wait_ge(gu_used[5], E + OVER)
            sp.wait_ge(gu_used[5], E)
            sp.dma_start(final_row, final_norm.rearrange("(a n) -> a n", a=1).to_broadcast([P, D])).then_inc(final_landed, 16)
            for t in range(NT):
                sp.wait_ge(out_ready, t + 1)
                sp.dma_start(out_v[:, t, :], x_sb[:, t, :]).then_inc(out_saved, 16)
            sp.wait_ge(out_saved, 16 * NT)

        @block.gpsimd
        def _(pool):
            n = 0

            def made(ins):
                nonlocal n
                n += 1
                ins.then_inc(consts, 1)
                pool.wait_ge(consts, n)

            g = nc.gpsimd
            made(g.memset(ident, 0.0))
            made(g.affine_select(out=ident, in_=ident, compare_op=ALU.not_equal, fill=1.0, base=0,
                                 pattern=[[-1, P]], channel_multiplier=1))
            made(g.memset(mean_w, 1.0 / DG))
            made(g.memset(eps, EPS))
            made(g.memset(ones, 1.0))
            made(g.affine_select(out=before, in_=ones, compare_op=ALU.is_gt, fill=0.0, base=0,
                                 pattern=[[1, P]], channel_multiplier=-1))
            made(g.iota(iota64.rearrange("p (a b) -> p a b", a=2), [[0, 2], [1, SLOTS]], 0, 0,
                        allow_small_or_imprecise_dtypes=True))
            made(g.iota(pri4, [[-1, G]], G, 0, allow_small_or_imprecise_dtypes=True))
            made(g.iota(pri8, [[-1, EG]], EG, 0, allow_small_or_imprecise_dtypes=True))
            made(g.iota(e64, [[SLOTS, E]], 0, 0, allow_small_or_imprecise_dtypes=True))
            made(g.iota(thr, [[SLOTS, NSPLIT]], SLOTS, 0, allow_small_or_imprecise_dtypes=True))
            made(g.iota(nums, [[1, OVER]], 0, 0, allow_small_or_imprecise_dtypes=True))
            made(g.iota(asg[:, :, :, 0], [[P, NT], [0, 2]], 0, 1, allow_small_or_imprecise_dtypes=True))
            for t in range(NT):
                for q in (1, 3):
                    pool.wait_ge(ht_hi, 4 * t + q + 1)
                    full, hi, lo = (h[:, 4 * q:4 * q + 4, t * P:(t + 1) * P] for h in (h_full, h_hi, h_lo))
                    g.tensor_tensor(lo, full, hi.bitcast(F32), ALU.subtract)\
                        .then_inc(ht_lo_pool, 1)

            def split_low(u, s, q):
                pool.wait_ge(w_hi_ready, u + 1)
                pool.sem_inc(turns, 1)
                g.tensor_tensor(w_lo[s], w_raw[q], w_hi[s].bitcast(F32), ALU.subtract).then_inc(w_ready, 1)

            pool.wait_ge(x_sq, NT)
            pool.wait_ge(ht_ps, 4 * NT)
            pool.wait_ge(w_ready, 1)
            split_low(1, 1, 1)
            split_low(2, 0, 2)
            split_low(3, 1, 3)
            with pool.Fori(1, NCH) as i:
                for q in range(NU):
                    split_low(i * NU + q, q % 2, q)
            for n in range(3):
                pool.wait_ge(sq_ready, 4 * n + 4)
                for m in range(1, NH):
                    g.tensor_tensor(sq[:, 0, :], sq[:, 0, :], sq[:, m, :], ALU.add).then_inc(sq_summed, 1)
                    pool.wait_ge(sq_summed, 3 * n + m)
            pool.wait_ge(logits_ps, NT)
            g.iota(tokens, [[1, T]], 0, 0, allow_small_or_imprecise_dtypes=True).then_inc(tokens_ready, 1)

            def gather(e, b, first=False):
                pool.wait_ge(idx_ready, e + 1)
                if not first:
                    pool.wait_ge(hte_ps, e - 1)
                pool.sem_inc(turns, 1)
                g.indirect_dma_start(out=hg[b][0:SLOTS], out_offset=None, in_=h2_dram,
                                     in_offset=bass.IndirectOffsetOnAxis(ap=gidx[b][0:SLOTS], axis=0))\
                    .then_inc(rows_gathered[b], 16)

            for b in (0, 1):
                pool.wait_ge(h2_saved[b], 32)
            gather(0, 0, first=True)
            gather(1, 1, first=True)
            with pool.Fori(0, E // 2) as i:
                for b in (0, 1):
                    gather(i * 2 + (b + 2), b)
            n_over = pool.value_load(over_i[0:1, OVER:OVER + 1], min_val=0, max_val=OVER)
            with pool.If(n_over > 0):
                with pool.Fori(E // 2, (E + OVER) // 2) as i:
                    for b in (0, 1):
                        gather(i * 2 + (b + 2), b)
                for b in (0, 1):
                    pool.wait_ge(rows_gathered[b], 16 * ((E + OVER) // 2 + 1))
            for b in (0, 1):
                pool.wait_ge(rows_gathered[b], 16 * (E // 2 + 1))

        @block.scalar
        def _(ae):
            a = nc.scalar
            ae.wait_ge(consts, 4)
            for t in range(NT):
                ae.wait_ge(x_landed[t], 16)
                if t:
                    ae.wait_ge(x_sq, t)
                a.activation(junk, x_sb[:, t, :], ACT.Square, accum_out=stat[:, t:t + 1]).then_inc(x_sq, 1)
                for q in (1, 3):
                    ae.wait_ge(ht_ps, 4 * t + q + 1)
                    a.activation(h_full[:, 4 * q:4 * q + 4, t * P:(t + 1) * P],
                                 ps[:, (4 * t + q) % 8, :].rearrange("p (a b) -> p a b", a=4), ACT.Copy)\
                        .then_inc(ht_full, 1)
            ae.dma_start(dft, dft_seq.rearrange("c (t p) n -> p c t n", p=P)).then_inc(dft_landed, 16)
            ae.dma_start(dfth, dft_head).then_inc(dft_landed, 16)

            def gains(landed, q):
                ae.wait_ge(w_landed[q], landed)
                for k in range(UK):
                    c = C_MIX + UK * q + k
                    a.activation(w_raw[q][:, k, :], w_raw[q][:, k, :], ACT.Copy, scale=cols[:, c:c + 1])\
                        .then_inc(w_scaled, 1)

            ae.wait_ge(cols_ready, 1)
            gains(16, 0)
            gains(16, 1)
            ae.wait_ge(x_sq, NT)
            for t in range(NT):
                a.activation(stat[:, NT + t:NT + t + 1], stat[:, t:t + 1], ACT.Sqrt, bias=eps, scale=1.0 / D)\
                    .then_inc(x_rms, 1)
            gains(16, 2)
            gains(16, 3)
            with ae.Fori(1, NCH) as i:
                for q in range(NU):
                    gains(i * 16 + 16, q)

            ae.wait_ge(z_stored, Z_FREE + 28)
            ae.dma_start(wr[:, :, 0:G], w_group[0].rearrange("(p k) n -> p k n", k=KT)).then_inc(router_landed, 16)
            ae.dma_start(wr[:, :, G:], w_router[0].rearrange("(p k) n -> p k n", k=KT)).then_inc(router_landed, 16)
            ae.dma_start(bias36[:, 0:G], b_group.to_broadcast([P, G])).then_inc(router_landed, 16)
            ae.dma_start(bias36[:, G:], b_router.to_broadcast([P, E])).then_inc(router_landed, 16)
            for h in range(NH):
                a.activation(zT[:, 8 + h, :], zT[:, 8 + h, :], ACT.Gelu).then_inc(v_gelu, 1)
            for h in range(NH):
                a.activation(zT[:, 4 + h, :], zT[:, 4 + h, :], ACT.Gelu).then_inc(u_gelu, 1)
            for h in range(NH):
                ae.wait_ge(vq_ps, h + 1)
                a.activation(vq[:, h].rearrange("p n c -> p (n c)"), ps[:, 4 + h, :], ACT.Copy).then_inc(vq_stored, 1)
            for h in range(NH):
                ae.wait_ge(ft_ps, h + 1)
                a.activation(fT[:, h, :], ps[:, (h + 1) % 4, :], ACT.Copy).then_inc(ft_stored, 1)

            def squares(group, done, count):
                ae.wait_ge(done, count)
                if group_order.index(group):
                    ae.wait_ge(ms_ps, group_order.index(group))
                for m in range(NH):
                    a.activation(sq[:, m, :], yT[:, group * NH + m, :], ACT.Square).then_inc(sq_ready, 1)

            group_order = [2, 3, 1, 0]
            def rms(nth):
                ae.wait_ge(ms_ps, nth + 1)
                a.activation(rstd[:, nth, :], ps[:, 4 + nth, :], ACT.Sqrt, bias=eps).then_inc(rms_ready, 1)

            squares(2, conv_stored, 4)
            for g in range(NH):
                ae.wait_ge(pool_ps, g + 1)
                a.activation(yT[:, 12 + g, :], ps[:, g, :], ACT.Copy, scale=cols[:, C_SCALE + g:C_SCALE + g + 1])\
                    .then_inc(pool_stored, 1)
            squares(3, pool_stored, 4)
            for m in (0, 1):
                ae.wait_ge(yf_ps, m + 1)
                a.activation(yT[:, m, :], ps[:, m, :], ACT.Copy).then_inc(yf_stored, 1)
            squares(1, mix_stored, 4)
            rms(0)
            rms(1)
            for m in (2, 3):
                ae.wait_ge(yf_ps, m + 1)
                a.activation(yT[:, m, :], ps[:, m, :], ACT.Copy).then_inc(yf_stored, 1)
            squares(0, yf_stored, 4)
            rms(2)
            rms(3)

            def store_h2t(t):
                for q in (0, 1):
                    ae.wait_ge(h2t_ps, 4 * t + q + 1)
                    if t:
                        ae.wait_ge(logits_ps, t)
                    a.activation(h2T[:, 4 * q:4 * q + 4, :].rearrange("p a b -> p (a b)"), ps[:, 4 + q, :], ACT.Copy)\
                        .then_inc(h2t_act, 1)

            for n in range(4):
                for t in range(NT):
                    j = 4 * n + t
                    ae.wait_ge(x2_stored, j + 1)
                    if j >= 2:
                        ae.wait_ge(x2_sq, j - 1)
                    a.activation(junk2[j % 2], x_sb[:, t, n * 512:(n + 1) * 512], ACT.Square,
                                 accum_out=part[:, t, n:n + 1]).then_inc(x2_sq, 1)
                    if n == 3:
                        ae.wait_ge(x2_sum, t + 1)
                        a.activation(stat[:, 16 + t:17 + t], stat[:, 12 + t:13 + t], ACT.Sqrt, bias=eps, scale=1.0 / D)\
                            .then_inc(x2_rms, 1)
                        if t:
                            store_h2t(t - 1)
            store_h2t(NT - 1)
            ae.wait_ge(exp_in, 1)
            a.activation(lgm, lgm, ACT.Exp).then_inc(exp_out, 1)
            ae.wait_ge(exp_in, 2)
            a.activation(v4[:, 5, :], v4[:, 5, :], ACT.Exp).then_inc(exp_out, 1)

            def store_rows_T(e):
                ae.wait_ge(hte_ps, e + 1)
                a.activation(hTe.rearrange("p (a b) c -> p a (b c)", a=2), ps[:, 2:4, :], ACT.Copy).then_inc(hte_ready, 1)

            def store_down(i, b):
                c = FT * b + FT - 1
                ae.wait_ge(wd_used[c % DS], i * 3 + (c // DS + 1))
                a.activation(yb_half(b, b), ps[b * SLOTS:(b + 1) * SLOTS, 6:8, :], ACT.Copy).then_inc(yb_act, 1)

            def blocks(i, first=False):
                for b in (0, 1):
                    e = i * 2 + b
                    if b:
                        if not first:
                            ae.wait_ge(comb_ps, i * 8)
                        store_down(i, 0)
                    ae.wait_ge(gu_used[GUS - 2], e + 1)
                    a.activation(act, ps[:, 0, 0:HF], ACT.Silu).then_inc(silu_ready, 1)
                    store_rows_T(e + 1)
                store_down(i, 1)

            store_rows_T(0)
            blocks(0, first=True)
            with ae.Fori(1, E // 2) as i:
                blocks(i)
            ae.wait_ge(over_ready, 1)
            n_over = ae.value_load(over_i[0:1, OVER:OVER + 1], min_val=0, max_val=OVER)
            with ae.If(n_over > 0):
                with ae.Fori(E // 2, (E + OVER) // 2) as i:
                    blocks(i)
                ae.wait_ge(comb_added, 4 * (E + OVER))
            ae.wait_ge(comb_added, 4 * E - 6)

            for t in range(NT):
                ae.wait_ge(comb_added, 4 * E - 6 + 2 * t)
                a.activation(junk3[t], x_sb[:, t, :], ACT.Square, accum_out=stat[:, t:t + 1]).then_inc(f_sq, 1)
                ae.wait_ge(f_sq, t + 1)
                a.activation(stat[:, NT + t:NT + t + 1], stat[:, t:t + 1], ACT.Sqrt, bias=eps, scale=1.0 / D)\
                    .then_inc(f_rms, 1)

        @block.tensor
        def _(pe):
            t_ = nc.tensor
            pe.wait_ge(consts, 2)

            def transpose_x(t):
                pe.wait_ge(x_landed[t], 16)
                for q in range(4):
                    if t >= 2:
                        pe.wait_ge(ht_full if q % 2 else ht_lo_dve, 2 * (t - 2) + q // 2 + 1)
                    elif t == 1 and q == 3:
                        pe.wait_ge(cols_ready, 1)
                    for k in range(4):
                        c = (4 * q + k) * P
                        mm = t_.transpose(ps[:, (4 * t + q) % 8, k * P:(k + 1) * P], x_sb[:, t, c:c + P], ident)
                    mm.then_inc(ht_ps, 1)

            transpose_x(0)
            pe.wait_ge(rows_landed, 64)
            t_.transpose(ps[:, 7, 0:NCOL], rows[0:NCOL], ident[0:NCOL, 0:NCOL]).then_inc(cols_ps, 1)
            for t in range(1, NT):
                transpose_x(t)

            def unit(u, bank, q):
                s = q % 2
                pe.wait_ge(w_ready, u + 1)
                for m in range(4):
                    if q == 0:
                        pe.wait_ge(z_stored, u + (m + 1))
                    for kk in range(UK):
                        k = q * UK + kk
                        cols_m = slice(m * P, (m + 1) * P)
                        for w, h in ((w_hi, h_hi), (w_hi, h_lo), (w_lo, h_hi)):
                            mm = t_.matmul(ps[:, bank + m, :], w[s][:, kk, cols_m], h[:, k, :],
                                           start=(k == 0 and w is w_hi and h is h_hi), stop=(k == KT - 1 and w is w_lo))
                    if q == NU - 1 and m < 3:
                        mm.then_inc(z_ps, 1)
                mm.then_inc(w_used, 1)
                if q == NU - 1:
                    pe.wait_ge(w_used, u + 1)
                    pe.sem_inc(z_ps, 1)

            for q in range(NU):
                pe.wait_ge(ht_lo_pool if q % 2 else ht_lo_dve, 7 + q // 2)
                unit(q, 0, q)
                if q == 1:
                    pe.wait_ge(diag_ready, NT)
                    t_.matmul(ps[:, 7, :], ones, diag.rearrange("p a b -> p (a b)"), start=True, stop=True)\
                        .then_inc(rstd_ps, 1)
            with pe.Fori(0, (NCH - 1) // 2) as i:
                for j in (0, 1):
                    for q in range(NU):
                        unit(i * (2 * NU) + ((j + 1) * NU + q), 4 - 4 * j, q)

            pe.wait_ge(dft_landed, 32)
            for s in range(NT):
                if s < 2:
                    pe.wait_ge(z_stored, Z_FREE + 24)
                else:
                    pe.wait_ge(ab_stored, s - 1)
                for h in range(NH):
                    c = (h % 2) * 2 * HD
                    mm = t_.matmul(ps[:, 4 + 2 * (s % 2) + h // 2, c:c + 2 * HD], zT[:, h, s * P:(s + 1) * P], dfth,
                                   start=True, stop=True)
                mm.then_inc(ab_ps, 1)
            for h in range(NH):
                pe.wait_ge(v_gelu, h + 1)
                pe.wait_ge(ab_stored, 3 + h // 2)
                for n in range(NT):
                    mm = t_.transpose(ps[:, 4 + h, n * P:(n + 1) * P], zT[:, 8 + h, n * P:(n + 1) * P], ident)
                mm.then_inc(vq_ps, 1)
            pe.wait_ge(mixw_landed, 80)
            pe.wait_ge(z_stored, Z_FREE + 28)
            for h in range(NH):
                mm = t_.transpose(ps[:, 0, h * P:(h + 1) * P], ws_raw[:, h, :], ident)
            mm.then_inc(ws_ps, 1)
            pe.wait_ge(ab_stored, NT)
            for h in range(NH):
                if h == 3:
                    pe.wait_ge(ws_stored, 1)
                for c in (0, 1):
                    for s in range(NT):
                        mm = t_.matmul(ps[:, (h + 1) % 4, :], ab[:, s, h, c * HD:(c + 1) * HD], dft[:, c, s, :],
                                       start=(c == 0 and s == 0), stop=(c == 1 and s == NT - 1))
                mm.then_inc(ft_ps, 1)
            for h in range(NH):
                pe.wait_ge(vq_stored, h + 1)
                mm = t_.matmul(ps[:, 4 + h, :].rearrange("p (n q) -> p n q", n=NT), ones[0:1, :],
                               bsp[0:1, h:h + 1, :].to_broadcast([1, NT, P]), start=True, stop=False)
                for n in range(NT):
                    mm = t_.matmul(ps[:, 4 + h, n * P:(n + 1) * P], vq[:, h, n, :], wsT[:, h, :],
                                   start=False, stop=(n == NT - 1))
                mm.then_inc(mix_ps, 1)
            pe.wait_ge(ft_stored, NH)
            for g in range(NH):
                pe.wait_ge(pooled, g + 1)
                t_.matmul(ps[:, g, :], wp[:, g, :], zT[:, 24 + g, :], start=True, stop=True).then_inc(pool_ps, 1)

            def mean_square(nth):
                pe.wait_ge(mix_stored, nth + 1)
                if nth < 3:
                    pe.wait_ge(sq_summed, 3 * nth + 3)
                    t_.matmul(ps[:, 4 + nth, :], mean_w, sq[:, 0, :], start=True, stop=True).then_inc(ms_ps, 1)
                    return
                for m in range(NH):
                    pe.wait_ge(sq_ready, 4 * nth + m + 1)
                    mm = t_.matmul(ps[:, 4 + nth, :], mean_w, sq[:, m, :], start=(m == 0), stop=(m == NH - 1))
                mm.then_inc(ms_ps, 1)

            def fourier_out(m):
                pe.wait_ge(pool_stored, m + 1)
                for k in range(NH):
                    mm = t_.matmul(ps[:, m, :], wf[:, k, m * P:(m + 1) * P], fT[:, k, :],
                                   start=(k == 0), stop=(k == NH - 1))
                mm.then_inc(yf_ps, 1)

            fourier_out(0)
            mean_square(0)
            fourier_out(1)
            mean_square(1)
            fourier_out(2)
            fourier_out(3)
            mean_square(2)
            mean_square(3)

            order = [*range(8, 12), *range(12, 16), *range(4, 8), *range(0, 4)]

            def out_tile(n, t):
                j = 4 * n + t
                if j >= 3:
                    pe.wait_ge(x2_stored, j - 2)
                for m, k in enumerate(order):
                    if j == 0:
                        pe.wait_ge(y_normed, m + 1)
                    mm = t_.matmul(ps[:, j % 3, :], yT[:, k, t * P:(t + 1) * P], wbuf[n % 2][:, k, :],
                                   start=(m == 0), stop=(m == KT - 1))
                mm.then_inc(xo_ps, 1)

            def transpose_h2(t):
                pe.wait_ge(h2_ready, t + 1)
                for q in range(4):
                    if t:
                        pe.wait_ge(h2t_act if q < 2 else h2t_dve, 2 * t - 1 + q % 2)
                    for k in range(4):
                        c = (4 * q + k) * P
                        mm = t_.transpose(ps[:, 4 + q, k * P:(k + 1) * P], h2[t % 2][:, c:c + P], ident)
                    mm.then_inc(h2t_ps, 1)

            def router(t):
                for k in range(KT):
                    if k == 0:
                        pe.wait_ge(h2t_act, 2 * t + 2)
                    if k == 8:
                        pe.wait_ge(h2t_dve, 2 * t + 2)
                    mm = t_.matmul(ps[:, 3, t * 64:t * 64 + G + E], h2T[:, k, :], wr[:, k, :],
                                   start=(k == 0), stop=(k == KT - 1))
                mm.then_inc(logits_ps, 1)

            pe.wait_ge(yf_stored, NH)
            for n in range(3):
                pe.wait_ge(wout_landed[n % 2], 16 * (n // 2 + 1))
                for t in range(NT):
                    out_tile(n, t)
            pe.wait_ge(wout_landed[1], 32)
            pe.wait_ge(router_landed, 64)
            pe.wait_ge(y_normed, MIX_TILES)
            for t in range(NT):
                out_tile(3, t)
                if t > 1:
                    router(t - 2)
                if t:
                    transpose_h2(t - 1)
            router(NT - 2)
            transpose_h2(NT - 1)
            router(NT - 1)
            pe.wait_ge(routed, 1)
            t_.matmul(ps[:, 0, 0:NT * E], before, A.rearrange("p a b -> p (a b)"), start=True, stop=True)
            t_.matmul(ps[:, 1, 0:NT * E], ones, A.rearrange("p a b -> p (a b)"), start=True, stop=True)\
                .then_inc(counted, 1)

            def plan(e):
                pe.wait_ge(pick_ready, e + 1)
                for j in range(NA):
                    mm = t_.matmul(ps[:, 5, 0:2], pick[:, j, :], asg[:, j // 2, j % 2, :],
                                   start=(j == 0), stop=(j == NA - 1))
                mm.then_inc(plan_ps, 1)

            def transpose_rows(e, i, b):
                pe.wait_ge(rows_gathered[b], i * 16 + 16)
                pe.sem_inc(turns, 1)
                for k in range(KT):
                    c = (k % 8) * SLOTS
                    mm = t_.transpose(ps[:, 2 + k // 8, c:c + SLOTS], hg[b][0:SLOTS, k * P:(k + 1) * P],
                                      ident[0:SLOTS, 0:SLOTS])
                mm.then_inc(hte_ps, 1)

            def combine(pair, t):
                if t == 0:
                    pe.wait_ge(yb_act, pair * 2 + 2)
                    pe.wait_ge(yb_dve, pair * 2 + 2)
                    pe.wait_ge(back_ready, pair + 1)
                for c in (0, 1):
                    if t:
                        pe.wait_ge(comb_added, pair * 8 + (2 * t - 1 + c))
                    for n in (2 * c, 2 * c + 1):
                        mm = t_.matmul(ps[:, 2 + n, :], back[:, t * P:(t + 1) * P], yb[:, n * 512:(n + 1) * 512],
                                       start=True, stop=True)
                    mm.then_inc(comb_ps, 1)

            def block_products(e, i, b, last):
                pe.wait_ge(hte_ready, e + 1)
                for q in range(NQ):
                    pe.wait_ge(gu_landed[2 * q], e * 16 + 16)
                    pe.wait_ge(gu_landed[2 * q + 1], e * 16 + 16)
                    for kk in range(QK):
                        k = q * QK + kk
                        for u in (0, 1):
                            for h in (0, 1):
                                mm = t_.matmul(ps[h * SLOTS:(h + 1) * SLOTS, u, 0:HF], hTe[:, k, :],
                                               gu[2 * q + u][:, kk, h * HF:(h + 1) * HF],
                                               start=(k == 0), stop=(k == KT - 1))
                            if kk == QK - 1:
                                mm.then_inc(gu_used[2 * q + u], 1)
                    if last is not None and q in (1, 2):
                        combine(last, 2 * b + q - 1)
                if last is not None:
                    pe.wait_ge(comb_added, last * 8 + (4 * b + 4))
                plan(e + 2)
                transpose_rows(e + 1, i + b, 1 - b)
                pe.wait_ge(act_ready, e + 1)
                for j in range(HF // P):
                    mm = t_.transpose(ps[:, 4, j * P:(j + 1) * P], act[:, j * P:(j + 1) * P], ident)
                mm.then_inc(at_ps, 1)
                pe.wait_ge(at_ready, e + 1)
                if b:
                    pe.wait_ge(yb_act, i * 2 + 1)
                    pe.wait_ge(yb_dve, i * 2 + 1)
                elif not isinstance(i, int):
                    pe.wait_ge(yb_act, i * 2)
                    pe.wait_ge(yb_dve, i * 2)
                for k in range(FT):
                    c = FT * b + k
                    s = c % DS
                    pe.wait_ge(wd_landed[s], i * 48 + 16 * (c // DS + 1))
                    h, j = divmod(k, HF // P)
                    for n in (0, 1):
                        for c in (0, 1):
                            mm = t_.matmul(ps[c * SLOTS:(c + 1) * SLOTS, 6 + n, :], aT[:, j, h * SLOTS:(h + 1) * SLOTS],
                                           wd[s][:, (2 * c + n) * 512:(2 * c + n + 1) * 512],
                                           start=(k == 0), stop=(k == FT - 1))
                    mm.then_inc(wd_used[s], 1)

            plan(0)
            pe.wait_ge(idx_ready, 1)
            plan(1)
            transpose_rows(0, 0, 0)
            block_products(0, 0, 0, None)
            block_products(1, 0, 1, None)
            with pe.Fori(1, E // 2) as i:
                for b in (0, 1):
                    block_products(i * 2 + b, i, b, i - 1)
            for t in range(NT):
                combine(E // 2 - 1, t)
            n_over = pe.value_load(over_i[0:1, OVER:OVER + 1], min_val=0, max_val=OVER)
            with pe.If(n_over > 0):
                with pe.Fori(E // 2, (E + OVER) // 2) as i:
                    pe.wait_ge(comb_added, i * 8)
                    for b in (0, 1):
                        block_products(i * 2 + b, i, b, None)
                    pe.wait_ge(idx_ready, i * 2 + 4)
                    for t in range(NT):
                        combine(i, t)
                pe.wait_ge(comb_added, 4 * (E + OVER))
            pe.wait_ge(comb_added, 4 * E)

        @block.vector
        def _(ve):
            v = nc.vector
            done = 0

            def then(ins):
                nonlocal done
                done += 1
                ins.then_inc(dve_done, 1)
                ve.wait_ge(dve_done, done)

            ve.wait_ge(cols_ps, 1)
            v.tensor_copy(cols, ps[:, 7, 0:NCOL]).then_inc(cols_ready, 1)
            ve.wait_ge(cols_ready, 1)

            def leading_bits(dst, src):
                return v.tensor_copy(dst, src)

            for t in range(NT):
                for q in range(4):
                    n = 4 * t + q + 1
                    hi, all_bits, lo = (h[:, 4 * q:4 * q + 4, t * P:(t + 1) * P] for h in (h_hi, h_full, h_lo))
                    if q % 2:
                        ve.wait_ge(ht_full, 2 * t + q // 2 + 1)
                        leading_bits(hi, all_bits).then_inc(ht_hi, 1)
                    else:
                        bank = ps[:, (4 * t + q) % 8, :].rearrange("p (a b) -> p a b", a=4)
                        ve.wait_ge(ht_ps, n)
                        leading_bits(hi, bank).then_inc(ht_hi, 1)
                        ve.wait_ge(ht_hi, n)
                        v.tensor_tensor(lo, bank, hi.bitcast(F32), ALU.subtract).then_inc(ht_lo_dve, 1)
            ve.sem_inc(z_stored, Z_FREE - 1)

            def split_high(u, s, q):
                ve.wait_ge(w_scaled, u * UK + UK)
                leading_bits(w_hi[s], w_raw[q]).then_inc(w_hi_ready, 1)

            def next_high(u, s, q):
                ve.wait_ge(w_used, u - 1)
                split_high(u, s, q)

            def store_z(chunk, bank):
                for m in range(4):
                    ve.wait_ge(z_ps, chunk * 4 + (m + 1))
                    if isinstance(chunk, int):
                        dst = zT[:, 4 * chunk + m, :]
                    else:
                        dst = zT[:, bass.ds(chunk * 4 + m, 1), :].rearrange("p a b -> p (a b)")
                    v.tensor_tensor(dst, ps[:, bank + m, :], rstd_x, ALU.mult).then_inc(z_stored, 1)

            ve.wait_ge(x_sq, 2)
            split_high(0, 0, 0)
            ve.wait_ge(w_hi_ready, 1)
            v.tensor_tensor(w_lo[0], w_raw[0], w_hi[0].bitcast(F32), ALU.subtract).then_inc(w_ready, 1)
            ve.wait_ge(x_sq, 3)
            split_high(1, 1, 1)
            for t in range(NT):
                ve.wait_ge(x_rms, t + 1)
                v.reciprocal(stat[:, 8 + t:9 + t], stat[:, NT + t:NT + t + 1]).then_inc(x_rinv, 1)
            for t in range(NT):
                ve.wait_ge(x_rinv, t + 1)
                v.tensor_scalar(diag[:, t, :], ident, stat[:, 8 + t:9 + t], None, ALU.mult).then_inc(diag_ready, 1)
            next_high(2, 0, 2)
            ve.wait_ge(rstd_ps, 1)
            v.tensor_copy(rstd_x, ps[:, 7, :]).then_inc(z_stored, 1)
            ve.wait_ge(z_stored, Z_FREE)
            for u in range(3, NU + 2):
                next_high(u, u % 2, u % NU)
            store_z(0, 0)
            with ve.Fori(0, (NCH - 3) // 2) as i:
                for j in (0, 1):
                    for q in range(NU):
                        next_high(i * (2 * NU) + ((j + 1) * NU + q + 2), q % 2, (q + 2) % NU)
                    store_z(i * 2 + (j + 1), 4 - 4 * j)
            for u in range(UNITS - NU - 2, UNITS - 2):
                next_high(u, u % 2, u % NU)
            store_z(NCH - 2, 4)
            for u in range(UNITS - 2, UNITS):
                next_high(u, u % 2, u % NU)
            store_z(NCH - 1, 0)

            for s in range(NT):
                ve.wait_ge(ab_ps, s + 1)
                bank = 4 + 2 * (s % 2)
                v.tensor_copy(ab[:, s].rearrange("p (a b) c -> p a (b c)", a=2), ps[:, bank:bank + 2, :])\
                    .then_inc(ab_stored, 1)
            ve.wait_ge(ws_ps, 1)
            v.tensor_copy(wsT.rearrange("p a b -> p (a b)"), ps[:, 0, :]).then_inc(ws_stored, 1)
            ve.wait_ge(z_stored, Z_FREE + 28)
            v.memset(conv_a[:, 0:1], 0.0)
            then(v.memset(conv_a[:, T + 1:T + 2], 0.0))
            for m in range(NH):
                tap = [cols[:, C_CONV + NH * j + m:C_CONV + NH * j + m + 1] for j in range(3)]
                then(v.tensor_tensor(conv_a[:, 1:T + 1], zT[:, 16 + m, :], zT[:, 20 + m, :], ALU.mult))
                then(v.tensor_scalar(conv_t, conv_a[:, 0:T], tap[0], None, ALU.mult))
                for j in (1, 2):
                    then(v.scalar_tensor_tensor(conv_t, conv_a[:, j:T + j], tap[j], conv_t, ALU.mult, ALU.add))
                v.tensor_tensor(yT[:, 8 + m, :], conv_t, zT[:, 12 + m, :], ALU.mult).then_inc(conv_stored, 1)
            v.memset(pool_in[:, 0:PAD], 0.0)
            v.memset(pool_in[:, PAD + T:], 0.0)
            for g, w in enumerate(WINDOWS):
                z = zT[:, 24 + g, :]
                then(v.tensor_copy(pool_in[:, PAD:PAD + T], z))
                src, width = pool_in, 1
                while width < w:
                    dst = pool_a if src is not pool_a else pool_b
                    n = POOLW - 2 * width + 1
                    then(v.tensor_tensor(dst[:, 0:n], src[:, 0:n], src[:, width:width + n], ALU.add))
                    src, width = dst, 2 * width
                o = PAD - w // 2
                then(v.tensor_tensor(src[:, o:o + w // 2], src[:, o:o + w // 2], edges[:, g, 0, 0:w // 2], ALU.mult))
                if w > 2:
                    r = o + T - w // 2 + 1
                    then(v.tensor_tensor(src[:, r:r + w // 2 - 1], src[:, r:r + w // 2 - 1],
                                         edges[:, g, 1, 0:w // 2 - 1], ALU.mult))
                v.scalar_tensor_tensor(z, src[:, o:o + T], 1.0 / w, z, ALU.mult, ALU.subtract).then_inc(pooled, 1)
            for h in range(NH):
                ve.wait_ge(mix_ps, h + 1)
                ve.wait_ge(u_gelu, h + 1)
                v.tensor_tensor(yT[:, 4 + h, :], ps[:, 4 + h, :], zT[:, 4 + h, :], ALU.mult).then_inc(mix_stored, 1)
            for n, (group, stored) in enumerate([(2, conv_stored), (3, pool_stored), (1, mix_stored), (0, yf_stored)]):
                ve.wait_ge(rms_ready, n + 1)
                ve.wait_ge(stored, NH)
                then(v.reciprocal(rstd[:, n, :], rstd[:, n, :]))
                for m in range(NH):
                    c = C_OUT + group * NH + m
                    v.scalar_tensor_tensor(yT[:, group * NH + m, :], yT[:, group * NH + m, :], cols[:, c:c + 1],
                                           rstd[:, n, :], ALU.mult, ALU.mult).then_inc(y_normed, 1)

            def store_h2t(t):
                for q in (2, 3):
                    ve.wait_ge(h2t_ps, 4 * t + q + 1)
                    if t:
                        ve.wait_ge(logits_ps, t)
                    v.tensor_copy(h2T[:, 4 * q:4 * q + 4, :].rearrange("p a b -> p (a b)"), ps[:, 4 + q, :])\
                        .then_inc(h2t_dve, 1)

            ve.wait_ge(x_back, 16)
            ve.wait_ge(ffn_landed, 16)
            for n in range(4):
                for t in range(NT):
                    j = 4 * n + t
                    ve.wait_ge(xo_ps, j + 1)
                    tile = x_sb[:, t, n * 512:(n + 1) * 512]
                    v.tensor_tensor(tile, ps[:, j % 3, :], tile, ALU.add).then_inc(x2_stored, 1)
                    if n == 3:
                        if t:
                            store_h2t(t - 1)
                        ve.wait_ge(x2_sq, 13 + t)
                        v.tensor_reduce(stat[:, 12 + t:13 + t], part[:, t, :], AX.X, ALU.add).then_inc(x2_sum, 1)
                        ve.wait_ge(x2_rms, t + 1)
                        v.reciprocal(stat[:, 20 + t:21 + t], stat[:, 16 + t:17 + t]).then_inc(x2_rinv, 1)
                        ve.wait_ge(x2_rinv, t + 1)
                        if t >= 2:
                            ve.wait_ge(h2_saved[t % 2], 16)
                            ve.wait_ge(h2t_ps, 4 * (t - 1))
                        v.scalar_tensor_tensor(h2[t % 2].rearrange("p (k c) -> p c k", k=KT),
                                               x_sb[:, t, :].rearrange("p (c k) -> p c k", k=KT), stat[:, 20 + t:21 + t],
                                               ffn_row.rearrange("p (c k) -> p c k", k=KT), ALU.mult, ALU.mult)\
                            .then_inc(h2_ready, 1)
            store_h2t(NT - 1)

            def col(n):
                return v4[:, n, :].rearrange("p (a b) -> p a b", b=1)

            def over_last(ap, *shape):
                return ap.to_broadcast([P, *shape])

            ve.wait_ge(logits_ps, NT)
            ve.wait_ge(router_landed, 64)
            ve.wait_ge(consts, 13)
            then(v.tensor_tensor(lg, ps[:, 3, 0:256].rearrange("p (a b) -> p a b", a=NT)[:, :, 0:G + E],
                                 bias36.rearrange("p (a b) -> p a b", a=1).to_broadcast([P, NT, G + E]), ALU.add))
            lgg = lg[:, :, 0:G]
            then(v.tensor_reduce(v4[:, 0, :], lgg, AX.X, ALU.max))
            v.tensor_tensor(lgm, lgg, over_last(col(0), NT, G), ALU.subtract).then_inc(exp_in, 1)
            then(v.tensor_tensor(ohg, lgg, over_last(col(0), NT, G), ALU.is_ge))
            then(v.tensor_tensor(r4, ohg, pri4.rearrange("p (a b) -> p a b", a=1).to_broadcast([P, NT, G]), ALU.mult))
            then(v.tensor_reduce(v4[:, 1, :], r4, AX.X, ALU.max))
            then(v.tensor_tensor(ohg, r4, over_last(col(1), NT, G), ALU.is_equal))
            ohg_b = ohg.rearrange("p a (b c) -> p a b c", c=1).to_broadcast([P, NT, G, EG])
            then(v.tensor_tensor(prod, lg[:, :, G:].rearrange("p a (b c) -> p a b c", b=G), ohg_b, ALU.mult))
            then(v.tensor_reduce(les, prod.rearrange("p a b c -> p a c b"), AX.X, ALU.add))
            pri8_b = pri8.rearrange("p (a b) -> p a b", a=1).to_broadcast([P, NT, EG])
            cur = les
            for k in (0, 1):
                m = 2 + 2 * k
                then(v.tensor_reduce(v4[:, m, :], cur, AX.X, ALU.max))
                then(v.tensor_tensor(r8, cur, over_last(col(m), NT, EG), ALU.is_ge))
                then(v.tensor_tensor(r8, r8, pri8_b, ALU.mult))
                then(v.tensor_reduce(v4[:, m + 1 if k == 0 else 6, :], r8, AX.X, ALU.max))
                then(v.tensor_tensor(oh[:, k], r8, over_last(col(m + 1 if k == 0 else 6), NT, EG), ALU.is_equal))
                if k == 0:
                    then(v.scalar_tensor_tensor(les2, oh[:, 0], -BIG, les, ALU.mult, ALU.add))
                    cur = les2
            v.tensor_tensor(v4[:, 5, :], v4[:, 4, :], v4[:, 2, :], ALU.subtract).then_inc(exp_in, 1)
            for k in (0, 1):
                then(v.tensor_tensor(full[:, k].rearrange("p a (b c) -> p a b c", b=G),
                                     oh[:, k].rearrange("p a (b c) -> p a b c", b=1).to_broadcast([P, NT, G, EG]),
                                     ohg_b, ALU.mult))
            v.tensor_tensor(A, full[:, 0], full[:, 1], ALU.add).then_inc(routed, 1)
            ve.wait_ge(exp_out, 2)
            then(v.tensor_reduce(v4[:, 7, :], lgm, AX.X, ALU.add))
            then(v.tensor_scalar(v4[:, 8, :], v4[:, 5, :], 1.0, None, ALU.add))
            then(v.tensor_tensor(v4[:, 9, :], v4[:, 7, :], v4[:, 8, :], ALU.mult))
            then(v.reciprocal(asg[:, :, 0, 1], v4[:, 9, :]))
            then(v.tensor_tensor(asg[:, :, 1, 1], asg[:, :, 0, 1], v4[:, 5, :], ALU.mult))
            ve.wait_ge(counted, 1)
            then(v.tensor_copy(tot.rearrange("p a b -> p (a b)"), ps[:, 1, 0:NT * E]))
            for t in range(1, NT):
                then(v.tensor_tensor(tot[:, t, :], tot[:, t - 1, :], tot[:, t, :], ALU.add))
            then(v.tensor_copy(Q.rearrange("p a b -> p (a b)"), ps[:, 0, 0:NT * E]))
            then(v.tensor_tensor(Q[:, 1:NT, :], Q[:, 1:NT, :], tot[:, 0:NT - 1, :], ALU.add))
            then(v.tensor_tensor(split_cmp, tot[:, NT - 1, :].rearrange("p (a b) -> p a b", b=1)
                                 .to_broadcast([P, E, NSPLIT]),
                                 thr.rearrange("p (a b) -> p a b", a=1).to_broadcast([P, E, NSPLIT]), ALU.is_gt))
            then(v.tensor_reduce(extra, split_cmp, AX.X, ALU.add))
            then(v.memset(zero32, 0.0))
            then(v.tensor_tensor_scan(over_end, zero32, extra, 0.0, ALU.add, ALU.add))
            then(v.tensor_tensor(over_v, over_end, extra, ALU.subtract))
            then(v.tensor_scalar(over_v, over_v, float(SLOTS), float(SLOTS * (E - 1)), ALU.mult, ALU.add))
            then(v.tensor_tensor(over_v, over_v, e64, ALU.subtract))
            then(v.tensor_scalar(t1, Q, float(SLOTS), None, ALU.is_ge))
            then(v.tensor_tensor(t1, t1, over_v.rearrange("p (a b) -> p a b", a=1).to_broadcast([P, NT, E]), ALU.mult))
            then(v.tensor_tensor(Q, Q, t1, ALU.add))
            then(v.tensor_tensor(Q, Q, e64.rearrange("p (a b) -> p a b", a=1).to_broadcast([P, NT, E]), ALU.add))
            for k in (0, 1):
                then(v.tensor_tensor(full[:, k], full[:, k], Q, ALU.mult))
                then(v.tensor_reduce(slot[:, :, k], full[:, k], AX.X, ALU.add))

            def compare():
                v.tensor_tensor(pick, iota64.rearrange("p (a b) -> p a b", a=1).to_broadcast([P, NA, P]),
                                slot.rearrange("p a (b c) -> p (a b) c", c=1).to_broadcast([P, NA, P]),
                                ALU.is_equal).then_inc(pick_ready, 1)

            def next_compare(e):
                v.tensor_scalar(slot, slot, -float(SLOTS), None, ALU.add).then_inc(slots_shifted, 1)
                ve.wait_ge(slots_shifted, e)
                compare()

            def read_plan(e, b):
                ve.wait_ge(plan_ps, e + 1)
                r = slice(b * SLOTS, (b + 1) * SLOTS)
                v.tensor_copy(held_next[r], ps[r, 5, 0:2])
                v.tensor_copy(gidx[b], ps[:, 5, 0:1]).then_inc(idx_ready, 1)

            def keep_plan(pair):
                ve.wait_ge(idx_ready, pair * 2 + 2)
                v.tensor_copy(held, held_next).then_inc(plan_kept, 1)

            def add_rows(pair, t):
                for c in (0, 1):
                    ve.wait_ge(comb_ps, pair * 8 + (2 * t + c + 1))
                    tile = x_sb[:, t, c * 1024:(c + 1) * 1024].rearrange("p (a b) -> p a b", a=2)
                    v.tensor_tensor(tile, ps[:, 2 + 2 * c:4 + 2 * c, :], tile, ALU.add).then_inc(comb_added, 1)

            def store_down(i, b):
                c = FT * b + FT - 1
                ve.wait_ge(wd_used[c % DS], i * 3 + (c // DS + 1))
                h = 1 - b
                v.tensor_copy(yb_half(b, h), ps[h * SLOTS:(h + 1) * SLOTS, 6:8, :]).then_inc(yb_dve, 1)

            def block_steps(e, i, b, last):
                if last is not None:
                    add_rows(last, 2 * b)
                    add_rows(last, 2 * b + 1)
                if b:
                    ve.wait_ge(plan_kept, i + 1)
                    v.tensor_scalar(back, tokens, held[:, 0:1], held[:, 1:2], ALU.is_equal, ALU.mult)\
                        .then_inc(back_ready, 1)
                    store_down(i, 0)
                ve.wait_ge(gu_used[GUS - 1], e + 1)
                ve.wait_ge(silu_ready, e + 1)
                v.tensor_tensor(act, ps[:, 1, 0:HF], act, ALU.mult).then_inc(act_ready, 1)
                if not b:
                    ve.wait_ge(plan_kept, i + 1)
                read_plan(e + 2, b)
                ve.wait_ge(at_ps, e + 1)
                v.tensor_copy(aT.rearrange("p a b -> p (a b)"), ps[:, 4, 0:HF]).then_inc(at_ready, 1)
                next_compare(e + 3)
                if b:
                    ve.wait_ge(back_ready, i + 1)
                    keep_plan(i + 1)
                    store_down(i, 1)

            compare()
            read_plan(0, 0)
            next_compare(1)
            read_plan(1, 1)
            next_compare(2)
            then(v.tensor_tensor(id_cmp, over_end.rearrange("p (a b) -> p a b", a=1).to_broadcast([P, OVER, E]),
                                 nums.rearrange("p (a b) -> p a b", b=1).to_broadcast([P, OVER, E]), ALU.is_le))
            then(v.tensor_reduce(over_f[:, 0:OVER], id_cmp, AX.X, ALU.add))
            then(v.tensor_scalar(over_f[:, 0:OVER], over_f[:, 0:OVER], float(E - 1), None, ALU.min))
            then(v.tensor_copy(over_f[:, OVER:], over_end[:, E - 1:E]))
            v.tensor_copy(over_i, over_f).then_inc(over_ready, 1)
            ve.wait_ge(tokens_ready, 1)
            keep_plan(0)
            block_steps(0, 0, 0, None)
            block_steps(1, 0, 1, None)
            with ve.Fori(1, E // 2) as i:
                for b in (0, 1):
                    block_steps(i * 2 + b, i, b, i - 1)
            for t in range(NT):
                add_rows(E // 2 - 1, t)
            n_over = ve.value_load(over_i[0:1, OVER:OVER + 1], min_val=0, max_val=OVER)
            with ve.If(n_over > 0):
                with ve.Fori(E // 2, (E + OVER) // 2) as i:
                    for b in (0, 1):
                        block_steps(i * 2 + b, i, b, None)
                    for t in range(NT):
                        add_rows(i, t)
                ve.wait_ge(comb_added, 4 * (E + OVER))
            ve.wait_ge(comb_added, 4 * E)

            ve.wait_ge(final_landed, 16)
            for t in range(NT):
                ve.wait_ge(f_rms, t + 1)
                v.reciprocal(stat[:, 8 + t:9 + t], stat[:, NT + t:NT + t + 1]).then_inc(f_rinv, 1)
                ve.wait_ge(f_rinv, t + 1)
                v.scalar_tensor_tensor(x_sb[:, t, :], x_sb[:, t, :], stat[:, 8 + t:9 + t], final_row,
                                       ALU.mult, ALU.mult).then_inc(out_ready, 1)


_INS = ["x", "mix_norm", "w_in", "w_fourier", "w_spatial", "b_spatial", "conv_w", "w_pool", "pool_scale", "out_norm",
        "w_out", "ffn_norm", "w_group", "b_group", "w_router", "b_router", "w_gate", "w_up", "w_down", "final_norm"]


def tables():
    n = np.arange(T)
    seq = 2 * np.pi * (np.outer(n, n) % T) / T
    m = np.arange(HD)
    head = 2 * np.pi * (np.outer(m, m) % HD) / HD
    scale = 1.0 / np.sqrt(T * HD)
    edge = np.ones((NH, 2, PAD))
    for g, w in enumerate(WINDOWS):
        for j in range(w // 2):
            edge[g, 0, j] = w / (j + w // 2)
            edge[g, 1, j] = w / (w - 1 - j)
    return {
        "dft_seq": np.stack([np.cos(seq), np.sin(seq)]).astype(np.float32),
        "dft_head": np.concatenate([np.cos(head) * scale, -np.sin(head) * scale], axis=1).astype(np.float32),
        "edge_scale": np.tile(edge.reshape(1, -1), (P, 1)).astype(np.float32),
    }


def kernel(**inputs):
    import concourse.bacc as bacc
    from concourse.bass_utils import run_bass_kernel_spmd

    nc = bacc.Bacc("TRN2", target_bir_lowering=False, num_devices=1)
    arrays, args = {}, []
    given = {name: np.ascontiguousarray(inputs[name]) for name in _INS}
    for name, a in {**given, **tables()}.items():
        arrays[f"in_{name}"] = a
        args.append(nc.dram_tensor(f"in_{name}", a.shape, mybir.dt.from_np(a.dtype), kind="ExternalInput").ap())
    args.append(nc.dram_tensor("out_0", (1, T, D), F32, kind="ExternalOutput").ap())
    build(nc, *args)
    r = run_bass_kernel_spmd(nc, [arrays], core_ids=[0])
    return r.results[0]["out_0"]
```
